# Optimizing a Trainium2 kernel written in Bass

```python
import math
import jax, jax.numpy as jnp
from jax import lax
import numpy as np

D_MODEL = 2048
BATCH = 1
SEQ = 256
DEPTH = 1

CHUNK = 64
N_MEM = 256

POOL_WINDOWS = (2, 4, 8, 16)
POOL_GROUPS = len(POOL_WINDOWS)
POOL_WIDTH = D_MODEL
POOL_GROUP_DIM = POOL_WIDTH // POOL_GROUPS

SSD_EXPAND = 2
SSD_INNER = SSD_EXPAND * D_MODEL
SSD_HEAD_DIM = 64
SSD_HEADS = SSD_INNER // SSD_HEAD_DIM
SSD_GROUPS = 8
SSD_STATE = 128
SSD_CONV = 4
SSD_CONV_DIM = SSD_INNER + 2 * SSD_GROUPS * SSD_STATE

N_BRANCH = 2
IN_COLS = POOL_WIDTH + SSD_INNER + SSD_CONV_DIM + SSD_HEADS + N_BRANCH * D_MODEL

X_HEADS = 4
X_HEAD_DIM = 128
X_WIDTH = X_HEADS * X_HEAD_DIM

D_FF = 5632

EPS = 1e-6

kernel_name = "hybrid_pool_ssd_macaron_sandwich_block"

def rms_norm(x, g):
    xf = x.astype(jnp.float32)
    y = xf * lax.rsqrt(jnp.mean(xf * xf, axis=-1, keepdims=True) + EPS)
    return (y * g.astype(jnp.float32)).astype(x.dtype)

def swiglu(u, w1, w3, w2):
    return (jax.nn.silu(u @ w1) * (u @ w3)) @ w2

def pool_mixer(p, pool_w, pool_scale):
    b, s, _ = p.shape
    pg = p.reshape(b, s, POOL_GROUPS, POOL_GROUP_DIM)
    cs = jnp.cumsum(pg.astype(jnp.float32), axis=1)
    cs0 = jnp.concatenate([jnp.zeros_like(cs[:, :1]), cs], axis=1)
    t = jnp.arange(s)
    outs = []
    for gi, w in enumerate(POOL_WINDOWS):
        lo = jnp.maximum(t + 1 - w, 0)
        win = cs0[:, 1:, gi] - cs0[:, lo, gi]
        cnt = (t + 1 - lo).astype(jnp.float32)[None, :, None]
        outs.append(win / cnt - pg[:, :, gi].astype(jnp.float32))
    pooled = jnp.stack(outs, axis=2).astype(p.dtype)
    mixed = jnp.einsum('bsgc,gcd->bsgd', pooled, pool_w).reshape(b, s, POOL_WIDTH)
    return mixed * pool_scale

def causal_depthwise_conv(u, w, bias):
    out = lax.conv_general_dilated(
        u, w[:, None, :].astype(u.dtype), window_strides=(1,), padding=[(SSD_CONV - 1, 0)],
        dimension_numbers=('NWC', 'WIO', 'NWC'), feature_group_count=u.shape[-1])
    return out + bias

def ssd_scan(xh, dt, A, Bm, Cm):
    b, s, h, p = xh.shape
    g, n = Bm.shape[2], Bm.shape[3]
    r = h // g
    c = s // CHUNK
    X = (xh * dt[..., None]).reshape(b, c, CHUNK, g, r, p)
    a = (dt * A).reshape(b, c, CHUNK, g, r)
    a_cs = jnp.cumsum(a, axis=2)
    Bc = Bm.reshape(b, c, CHUNK, g, n)
    Cc = Cm.reshape(b, c, CHUNK, g, n)
    seg = a_cs[:, :, :, None] - a_cs[:, :, None, :]
    mask = jnp.tril(jnp.ones((CHUNK, CHUNK), dtype=bool))[None, None, :, :, None, None]
    Lmat = jnp.exp(jnp.where(mask, seg, -jnp.inf))
    CB = jnp.einsum('bclgn,bcsgn->bclsg', Cc, Bc)
    y_diag = jnp.einsum('bclsg,bclsgr,bcsgrp->bclgrp', CB, Lmat, X)
    decay_states = jnp.exp(a_cs[:, :, -1:] - a_cs)
    states = jnp.einsum('bclgn,bclgr,bclgrp->bcgrpn', Bc, decay_states, X)
    chunk_decay = jnp.exp(a_cs[:, :, -1])

    def step(carry, inp):
        st, dec = inp
        return carry * dec[..., None, None] + st, carry

    init = jnp.zeros((b, g, r, p, n), dtype=states.dtype)
    _, prev = lax.scan(step, init, (jnp.moveaxis(states, 1, 0), jnp.moveaxis(chunk_decay, 1, 0)))
    prev = jnp.moveaxis(prev, 0, 1)
    y_off = jnp.einsum('bclgn,bcgrpn,bclgr->bclgrp', Cc, prev, jnp.exp(a_cs))
    return (y_diag + y_off).reshape(b, s, h, p)

def ssd_mixer(z, xbc, dt_raw, conv_w, conv_b, dt_bias, a_log, d_skip, norm_g):
    b, s, _ = z.shape
    xbc = jax.nn.silu(causal_depthwise_conv(xbc, conv_w, conv_b))
    xs = xbc[..., :SSD_INNER].reshape(b, s, SSD_HEADS, SSD_HEAD_DIM)
    Bm = xbc[..., SSD_INNER:SSD_INNER + SSD_GROUPS * SSD_STATE].reshape(b, s, SSD_GROUPS, SSD_STATE)
    Cm = xbc[..., SSD_INNER + SSD_GROUPS * SSD_STATE:].reshape(b, s, SSD_GROUPS, SSD_STATE)
    dt = jax.nn.softplus(dt_raw.astype(jnp.float32) + dt_bias.astype(jnp.float32))
    A = -jnp.exp(a_log.astype(jnp.float32))
    y = ssd_scan(xs, dt, A, Bm, Cm) + d_skip.astype(jnp.float32)[:, None] * xs.astype(jnp.float32)
    y = y.reshape(b, s, SSD_INNER).astype(z.dtype) * jax.nn.silu(z)
    y = rms_norm(y.reshape(b, s, SSD_GROUPS, SSD_INNER // SSD_GROUPS),
                 norm_g.reshape(SSD_GROUPS, SSD_INNER // SSD_GROUPS))
    return y.reshape(b, s, SSD_INNER)

def memory_cross_attention(u, mem_n, w_q, w_k, w_v, w_o):
    b, s, _ = u.shape
    q = (u @ w_q).reshape(b, s, X_HEADS, X_HEAD_DIM)
    k = (mem_n @ w_k).reshape(b, N_MEM, X_HEADS, X_HEAD_DIM)
    v = (mem_n @ w_v).reshape(b, N_MEM, X_HEADS, X_HEAD_DIM)
    sc = jnp.einsum('bshd,bmhd->bhsm', q, k).astype(jnp.float32) / math.sqrt(X_HEAD_DIM)
    pr = jax.nn.softmax(sc, axis=-1).astype(v.dtype)
    o = jnp.einsum('bhsm,bmhd->bshd', pr, v).reshape(b, s, X_WIDTH)
    return o @ w_o

def setup_inputs(seed: int = 0) -> dict:
    key = jax.random.key(seed)
    ks = iter(jax.random.split(key, 64))
    f32 = jnp.float32
    L = DEPTH

    def nrm(shape, fan_in):
        return jax.random.normal(next(ks), shape, f32) * (fan_in ** -0.5)

    def gain(shape):
        return 1.0 + 0.02 * jax.random.normal(next(ks), shape, f32)

    def small(shape):
        return 0.02 * jax.random.normal(next(ks), shape, f32)

    x = jax.random.normal(next(ks), (BATCH, SEQ, D_MODEL), f32)
    mem = jax.random.normal(next(ks), (BATCH, N_MEM, D_MODEL), f32)
    dt0 = jnp.exp(jax.random.uniform(next(ks), (L, SSD_HEADS), f32) * (math.log(0.1) - math.log(0.001))
                  + math.log(0.001))
    dt0 = jnp.maximum(dt0, 1e-4)
    dt_bias = dt0 + jnp.log(-jnp.expm1(-dt0))
    a_log = jnp.log(jax.random.uniform(next(ks), (L, SSD_HEADS), f32, 1.0, 16.0))
    return {
        "x": x,
        "mem": mem,
        "ffn1_pre_g": gain((L, D_MODEL)),
        "ffn1_w1": nrm((L, D_MODEL, D_FF), D_MODEL),
        "ffn1_w3": nrm((L, D_MODEL, D_FF), D_MODEL),
        "ffn1_w2": nrm((L, D_FF, D_MODEL), D_FF),
        "ffn1_post_g": gain((L, D_MODEL)),
        "mix_pre_g": gain((L, D_MODEL)),
        "w_in": nrm((L, D_MODEL, IN_COLS), D_MODEL),
        "b_gate": small((L, N_BRANCH * D_MODEL)),
        "pool_w": nrm((L, POOL_GROUPS, POOL_GROUP_DIM, POOL_GROUP_DIM), POOL_GROUP_DIM),
        "pool_scale": gain((L, POOL_WIDTH)),
        "w_pool_out": nrm((L, POOL_WIDTH, D_MODEL), POOL_WIDTH),
        "conv_w": nrm((L, SSD_CONV, SSD_CONV_DIM), SSD_CONV),
        "conv_b": small((L, SSD_CONV_DIM)),
        "dt_bias": dt_bias,
        "a_log": a_log,
        "d_skip": gain((L, SSD_HEADS)),
        "ssd_norm_g": gain((L, SSD_INNER)),
        "w_ssd_out": nrm((L, SSD_INNER, D_MODEL), SSD_INNER),
        "w_mix_out": nrm((L, D_MODEL, D_MODEL), D_MODEL),
        "mix_post_g": gain((L, D_MODEL)),
        "xattn_pre_g": gain((L, D_MODEL)),
        "mem_norm_g": gain((L, D_MODEL)),
        "w_q": nrm((L, D_MODEL, X_WIDTH), D_MODEL),
        "w_k": nrm((L, D_MODEL, X_WIDTH), D_MODEL),
        "w_v": nrm((L, D_MODEL, X_WIDTH), D_MODEL),
        "w_xo": nrm((L, X_WIDTH, D_MODEL), X_WIDTH),
        "xattn_post_g": gain((L, D_MODEL)),
        "ffn2_pre_g": gain((L, D_MODEL)),
        "ffn2_w1": nrm((L, D_MODEL, D_FF), D_MODEL),
        "ffn2_w3": nrm((L, D_MODEL, D_FF), D_MODEL),
        "ffn2_w2": nrm((L, D_FF, D_MODEL), D_FF),
        "ffn2_post_g": gain((L, D_MODEL)),
    }

def reference(x, mem, ffn1_pre_g, ffn1_w1, ffn1_w3, ffn1_w2, ffn1_post_g, mix_pre_g, w_in, b_gate,
              pool_w, pool_scale, w_pool_out, conv_w, conv_b, dt_bias, a_log, d_skip, ssd_norm_g,
              w_ssd_out, w_mix_out, mix_post_g, xattn_pre_g, mem_norm_g, w_q, w_k, w_v, w_xo,
              xattn_post_g, ffn2_pre_g, ffn2_w1, ffn2_w3, ffn2_w2, ffn2_post_g):
    h = x
    c0 = POOL_WIDTH
    c1 = c0 + SSD_INNER
    c2 = c1 + SSD_CONV_DIM
    c3 = c2 + SSD_HEADS
    for i in range(DEPTH):
        f = swiglu(rms_norm(h, ffn1_pre_g[i]), ffn1_w1[i], ffn1_w3[i], ffn1_w2[i])
        h = h + 0.5 * rms_norm(f, ffn1_post_g[i])

        u = rms_norm(h, mix_pre_g[i])
        proj = u @ w_in[i]
        p_in, z, xbc, dt_raw = proj[..., :c0], proj[..., c0:c1], proj[..., c1:c2], proj[..., c2:c3]
        gates = jax.nn.sigmoid(proj[..., c3:] + b_gate[i])
        g_a, g_b = gates[..., :D_MODEL], gates[..., D_MODEL:]
        y_a = pool_mixer(p_in, pool_w[i], pool_scale[i]) @ w_pool_out[i]
        y_b = ssd_mixer(z, xbc, dt_raw, conv_w[i], conv_b[i], dt_bias[i], a_log[i], d_skip[i],
                        ssd_norm_g[i]) @ w_ssd_out[i]
        mixed = (g_a * y_a + g_b * y_b) @ w_mix_out[i]
        h = h + rms_norm(mixed, mix_post_g[i])

        mem_n = rms_norm(mem, mem_norm_g[i])
        a = memory_cross_attention(rms_norm(h, xattn_pre_g[i]), mem_n, w_q[i], w_k[i], w_v[i], w_xo[i])
        h = h + rms_norm(a, xattn_post_g[i])

        f = swiglu(rms_norm(h, ffn2_pre_g[i]), ffn2_w1[i], ffn2_w3[i], ffn2_w2[i])
        h = h + 0.5 * rms_norm(f, ffn2_post_g[i])
    return h


_drawn_inputs = setup_inputs


def setup_inputs(seed=0):
    import zlib

    import numpy as np

    out = dict(_drawn_inputs(seed))
    spreads = {}
    factors = {'ffn1_pre_g': 3.689,
     'ffn1_post_g': 5.275,
     'mix_pre_g': 2.977,
     'b_gate': 8.0,
     'pool_scale': 6.095,
     'conv_b': 3.957,
     'd_skip': 64.0,
     'ssd_norm_g': 15.491,
     'mix_post_g': 4.033,
     'xattn_pre_g': 4.995,
     'mem_norm_g': 3.482,
     'xattn_post_g': 16.718,
     'ffn2_pre_g': 29.428,
     'ffn2_post_g': 45.193}
    for name, (base, spread) in spreads.items():
        noise = np.random.default_rng([zlib.crc32(name.encode()), seed]).standard_normal(out[name].shape)
        drawn = base * np.exp(spread * noise) if base else spread * noise
        out[name] = __import__('jax').numpy.asarray(drawn.astype(out[name].dtype))
    for name, factor in factors.items():
        out[name] = (out[name] * factor).astype(out[name].dtype)
    return out
```

```python
from contextlib import ExitStack

import concourse.bass as bass
from concourse import mybir

ALU = mybir.AluOpType
ACT = mybir.ActivationFunctionType
F32 = mybir.dt.float32
F32R = mybir.dt.float32r
BF16 = mybir.dt.bfloat16
AX = mybir.AxisListType

P = 128
RING = 4
AHEAD = 3
CK = 2
NCOL = 512
EPS = 1e-6
WINDOWS = (2, 4, 8, 16)
TAPS = 4
HEAD_DIM = 64
X_HEADS = 4

KB = 1024
BASE = 16512


def hybrid_block(nc, x, mem, ffn1_pre_g, ffn1_w1, ffn1_w3, ffn1_w2, ffn1_post_g, mix_pre_g, w_in, b_gate,
                 pool_w, pool_scale, w_pool_out, conv_w, conv_b, dt_bias, a_log, d_skip, ssd_norm_g,
                 w_ssd_out, w_mix_out, mix_post_g, xattn_pre_g, mem_norm_g, w_q, w_k, w_v, w_xo,
                 xattn_post_g, ffn2_pre_g, ffn2_w1, ffn2_w3, ffn2_w2, ffn2_post_g,
                 identity, causal, anticausal, inv_count, out):
    _, S, D = x.shape
    DFF = ffn1_w1.shape[2]
    INNER = w_ssd_out.shape[1]
    CONV = conv_w.shape[2]
    HEADS = dt_bias.shape[1]
    GROUPS = (CONV - INNER) // 2 // P
    HPG = HEADS // GROUPS
    T = S // P
    KD = D // P
    M = NCOL // P
    NJ = D // NCOL
    NP = DFF // NCOL
    CD = KD // CK
    CF = DFF // P // CK
    CI = INNER // P // CK
    CX = NCOL // P // CK
    WG = HPG * HEAD_DIM
    assert T == 2 and WG == NCOL and HPG == 8 and NP % 2 == 1 and (2 * CF) % RING == 0

    jobs = {}
    names = []

    def plan(name, chunks):
        start = jobs[names[-1]][1] + jobs[names[-1]][2] if names else 0
        jobs[name] = (len(names), start, chunks)
        names.append(name)

    def plan_ffn(f):
        for j in range(NP):
            plan(("gate", f, j), CD)
            plan(("up", f, j), CD)
        for j in range(NJ):
            plan(("down", f, j), CF)

    plan_ffn(0)
    for name, n in (("pin0", CD), ("dt", 1), ("pin1", CD), ("pw0", CX), ("pin2", CD), ("pw1", CX), ("pin3", CD),
                    ("pw2", CX), ("B0", CD), ("pw3", CX)):
        plan(name, n)
    for j in range(NJ):
        plan(("gate_a", j), CD)
        plan(("pool_out", j), CD)
    for name in ("C0", "B1", "C1"):
        plan(name, CD)
    for g in range(GROUPS):
        plan(("x", g), CD)
        plan(("z", g), CD)
    for j in range(NJ):
        plan(("gate_b", j), CD)
    for j in range(NJ):
        plan(("ssd_out", j), CI)
    for j in range(NJ):
        plan(("mix_out", j), CD)
    for name in ("k", "q", "v"):
        plan(name, CD)
    plan("attend", 0)
    for j in range(NJ):
        plan(("xo", j), CX)
    plan_ffn(1)
    NCH = jobs[names[-1]][1] + jobs[names[-1]][2]

    def number(name):
        return jobs[name][0]

    def first(name):
        return jobs[name][1]

    def end(name):
        return jobs[name][1] + jobs[name][2]

    def slot(name):
        return jobs[name][0] % 2

    def moved(name):
        return jobs[name][0] // 2 + 1

    row_users = [n for n in names if isinstance(n, tuple) and n[0] in ("down", "gate_a", "gate_b", "mix_out", "xo")]

    def row_count(name):
        return 1 + [n for n in row_users if slot(n) == slot(name)].index(name)

    areas = {0: [], 1: []}
    for kind in ("pre0",):
        for q in range(4):
            areas[q % 2].append((kind, q))
    areas[0] += [("hidden", 0, j) for j in range(NP)]
    for q in range(4):
        areas[q % 2].append(("pre1", q))
    areas[1] += ["cs", "csT", ("cb", 0), ("cb", 1), ("cb", 2), ("cb", 3)] + [("Y", g) for g in range(GROUPS)]
    for g in range(GROUPS):
        areas[0] += [("xT", g), ("yT", g)]
    areas[0] += [("merged", j) for j in range(NJ)] + [("mem", q) for q in range(4)]
    for q in range(4):
        areas[q % 2].append(("pre2", q))
    areas[0] += ["score0", "probT0"]
    areas[1] += ["score1", "probT1"]
    for q in range(4):
        areas[q % 2].append(("pre3", q))
    areas[0] += [("hidden", 1, j) for j in range(NP)]

    def use(k, name):
        return areas[k].index(name) + 1

    split_kinds = ("pre0", "pre1", "pre2", "pre3", "hidden", "merged", "mem")
    splits = {k: [n for n in areas[k] if isinstance(n, tuple) and n[0] in split_kinds] for k in (0, 1)}

    def high_use(k, name):
        return splits[k].index(name) + 1

    with ExitStack() as ctx:
        def at(name, kb, shape, dt=F32):
            return nc.alloc_sbuf_tensor_at(name, shape, dt, offset=BASE + int(kb * KB))

        raw = at("raw", 0, [P, RING, CK, NCOL])
        wh = at("wh", 16, [P, RING, CK, NCOL], F32R)
        wl = at("wl", 32, [P, RING, CK, NCOL], F32R)
        res = at("res", 48, [P, T, D])
        uh = at("uh", 64, [P, KD, S], F32R)
        ul = at("ul", 80, [P, KD, S], F32R)
        hidh = at("hidh", 96, [P, DFF // P, S], F32R)
        hidl = at("hidl", 140, [P, DFF // P, S], F32R)
        silu_g = at("silu_g", 184, [P, T, NCOL])
        hid = at("hid", 188, [P, T, NCOL])
        F = at("F", 184, [P, T, D])
        mixh = at("mixh", 96, [P, KD, S], F32R)
        mixl = at("mixl", 112, [P, KD, S], F32R)
        poolh = at("poolh", 128, [P, M, S], F32R)
        pooll = at("pooll", 132, [P, M, S], F32R)
        pool_x = at("pool_x", 148, [P, M, S])
        win_a = at("win_a", 152, [P, M, S])
        win_b = at("win_b", 156, [P, M, S])
        sig_a = at("sig_a", 160, [P, T, NCOL])
        invc = at("invc", 164, [P, 4, S])
        yn = at("yn", 96, [P, INNER // P, S])
        cbm = at("cbm", 128, [P, GROUPS, 3 * P])
        bT = at("bT", 140, [P, M, S])
        cT = at("cT", 144, [P, M, S])
        E = at("E", 140, [P, HPG, 3 * P])
        csb = at("csb", 152, [P, HPG, T, P])
        xc = at("xc", 160, [P, M, S])
        X = at("X", 164, [P, T, NCOL])
        Xdt = at("Xdt", 168, [P, T, NCOL])
        zs = at("zs", 172, [P, T, NCOL])
        yb = at("yb", 176, [P, T, NCOL])
        small = at("small", 180, [P, 16, HEADS])
        DTR, AB, EX, LG, DTV, AV, CS, REM = 0, 2, 4, 6, 8, 10, 12, 14
        EA = 15
        cst = at("cst", 168, [P, P])
        upper = at("upper", 169, [P, P])
        rows = at("rows", 168, [P, 4, P])
        dtb_bc = at("dtb_bc", 172, [P, HEADS])
        alog_bc = at("alog_bc", 172.25, [P, HEADS])
        ynh = at("ynh", 128, [P, INNER // P, S], F32R)
        ynl = at("ynl", 96, [P, INNER // P, S], F32R)
        sig_b = at("sig_b", 160, [P, T, D])
        memh = at("memh", 96, [P, KD, S], F32R)
        meml = at("meml", 112, [P, KD, S], F32R)
        memx = at("memx", 128, [P, T, D])
        mem_junk = at("mem_junk", 176, [P, D], BF16)
        kT = at("kT", 144, [P, M, S])
        V = at("V", 148, [P, T, NCOL])
        qT = at("qT", 152, [P, M, S])
        prob = at("prob", 156, [P, T, X_HEADS, S])
        probT = at("probT", 164, [P, T, X_HEADS, S])
        oh = at("oh", 172, [P, M, S], F32R)
        ol = at("ol", 176, [P, M, S], F32R)
        smax = at("smax", 180, [P, 4, T * X_HEADS])
        row_bc = at("row_bc", 200, [P, 2, NCOL])
        d_bc = at("d_bc", 204, [P, HEADS])
        ident = at("ident", 204.5, [P, P])
        tri = at("tri", 205, [P, P])
        cols = at("cols", 205.5, [P, 368])
        stat = at("stat", 206.9375, [P, 32])
        ssq_job = stat[:, 0:8].rearrange("p (t j) -> p t j", t=T)
        ssum, sv, ss, sr, ssq_res, sr_ffn = (stat[:, 8 + 2 * i:10 + 2 * i] for i in range(6))
        UPDATES = {1: T, 2: T, 3: NJ * T, 4: 2 * T}

        def updates_before(n):
            return sum(UPDATES[b] for b in UPDATES if b < n)

        G_COL = {"pre0": 0, "pre1": KD, "pre2": 2 * KD, "pre3": 3 * KD, "mem": 4 * KD}
        PS_COL, NG_COL, CW_COL, CB_COL = 5 * KD, 6 * KD, 8 * KD, 8 * KD + 192

        J = ctx.enter_context(nc.psum_tensor("J", [P, 2, T, NCOL], F32))
        A = ctx.enter_context(nc.psum_tensor("A", [P, 2, T, NCOL], F32))

        def tok(s):
            return J[:, s]

        def feat(s):
            return J[:, s].rearrange("p t (a n) -> p (t a) n", n=S)

        def area(k):
            return A[:, k].rearrange("p t (a n) -> p (t a) n", n=S)

        cs_dram = nc.dram_tensor("cs_dram", [T, HEADS, P], F32).ap()

        def sem(name):
            return ctx.enter_context(nc.semaphore(name))

        loaded = [sem(f"loaded{i}") for i in range(RING)]
        high = sem("high")
        low = sem("low")
        panels = sem("panels")
        used = sem("used")
        evacuated = [sem("evacuated0"), sem("evacuated1")]
        row_loaded = [sem("row_loaded0"), sem("row_loaded1")]
        t_ready = [sem("t_ready0"), sem("t_ready1")]
        t_high = [sem("t_high0"), sem("t_high1")]
        t_moved = [sem("t_moved0"), sem("t_moved1")]
        x_loaded = sem("x_loaded")
        rows_loaded = sem("rows_loaded")
        consts_loaded = sem("consts_loaded")
        cols_ready = sem("cols_ready")
        job_squares = sem("job_squares")
        res_ready = sem("res_ready")
        res_squares = sem("res_squares")
        var_ready = sem("var_ready")
        root_ready = sem("root_ready")
        normed = sem("normed")
        step = sem("step")
        mix_loaded = sem("mix_loaded")
        pooled_ready = sem("pooled_ready")
        pooled_high = sem("pooled_high")
        pooled_low = sem("pooled_low")
        pw_high = sem("pw_high")
        gate_biased = sem("gate_biased")
        gate_ready = sem("gate_ready")
        dt_step = sem("dt_step")
        dt_func = sem("dt_func")
        a_ready = sem("a_ready")
        cs_stored = sem("cs_stored")
        csb_loaded = sem("csb_loaded")
        bc_silu = sem("bc_silu")
        seg_ready = sem("seg_ready")
        exp_ready = sem("exp_ready")
        w_ready = sem("w_ready")
        xc_silu = sem("xc_silu")
        xdt_ready = sem("xdt_ready")
        gated = sem("gated")
        y_squares = sem("y_squares")
        y_normed = sem("y_normed")
        yn_high = sem("yn_high")
        yn_low = sem("yn_low")
        merged = sem("merged")
        mem_loaded = sem("mem_loaded")
        mem_squares = sem("mem_squares")
        mem_normed = sem("mem_normed")
        max_ready = sem("max_ready")
        probs = sem("probs")
        probs_scaled = sem("probs_scaled")
        o_high = sem("o_high")
        stored = sem("stored")

        def lin(static, i, per):
            return static if i is None else i * per + static

        def panel(w, k, col):
            return w[k * CK * P:(k + 1) * CK * P, col].rearrange("(k p) n -> p k n", p=P)

        C1 = D + INNER
        C3 = C1 + CONV + HEADS
        W_IN = w_in[0]

        block = ctx.enter_context(nc.Block())

        @block.sync
        def _(sp):
            sp.dma_start(ident[:], identity).then_inc(consts_loaded, 16)
            sp.dma_start(tri[:], causal).then_inc(consts_loaded, 16)
            for n, g in enumerate((ffn1_pre_g, mix_pre_g, xattn_pre_g, ffn2_pre_g, mem_norm_g, pool_scale)):
                sp.dma_start(rows[n * KD:(n + 1) * KD, 0, :], g[0].rearrange("(b p) -> b p", p=P)).then_inc(rows_loaded, 16)
            sp.dma_start(rows[6 * KD:8 * KD, 0, :], ssd_norm_g[0].rearrange("(b p) -> b p", p=P)).then_inc(rows_loaded, 16)
            cw = conv_w[0].rearrange("a (b p) -> (a b) p", p=P)
            nb = CONV // P
            for n in range(2):
                sp.dma_start(rows[0:2 * nb, 1 + n, :], cw[2 * nb * n:2 * nb * (n + 1), :]).then_inc(rows_loaded, 16)
            sp.dma_start(rows[0:nb, 3, :], conv_b[0].rearrange("(b p) -> b p", p=P)).then_inc(rows_loaded, 16)
            sp.dma_start(d_bc[:], d_skip[0:1, :].to_broadcast([P, HEADS])).then_inc(consts_loaded, 16)

            chunk = [0]

            def load(src, i=None, per=0, view=None, top=False):
                c = chunk[0]
                r = c % RING
                if i is not None or c >= RING:
                    sp.wait_ge(low, lin(c - RING + 1, i, per))
                if top and i is not None:
                    sp.sem_inc(panels, 1)
                dst = raw[:, r] if view is None else view(r)
                sp.dma_start(dst, src).then_inc(loaded[r], 16)
                chunk[0] += 1

            def load_job(w, col, n, i=None, per=0):
                for k in range(n):
                    load(panel(w, k, col), i, per, top=(k == 0))

            def ffn(f, w1, w3, w2):
                load_job(w1[0], slice(0, NCOL), CD)
                load_job(w3[0], slice(0, NCOL), CD)
                with sp.Fori(1, NP) as j:
                    chunk[0] = first(("gate", f, 0))
                    load_job(w1[0], bass.ds(j * NCOL, NCOL), CD, j, 2 * CD)
                    load_job(w3[0], bass.ds(j * NCOL, NCOL), CD, j, 2 * CD)
                chunk[0] = first(("down", f, 0))
                with sp.Fori(0, NJ // 2) as i:
                    for o in range(2):
                        col = bass.ds(i * (2 * NCOL) + o * NCOL, NCOL)
                        load_job(w2[0], col, CF, i, 2 * CF)
                chunk[0] = end(("down", f, NJ - 1))

            ffn(0, ffn1_w1, ffn1_w3, ffn1_w2)

            def cols_at(c):
                return slice(c, c + NCOL)

            for name in ("pin0", "dt", "pin1", "pw0", "pin2", "pw1", "pin3", "pw2", "B0", "pw3"):
                if name == "B0":
                    load_job(W_IN, cols_at(C1 + INNER), CD)
                elif name == "dt":
                    load(W_IN[:, C1 + CONV:C3].rearrange("(k p) n -> p k n", p=P),
                         view=lambda r: raw[:, r].rearrange("p k n -> p (k n)").rearrange("p (k n) -> p k n", n=HEADS))
                else:
                    g = int(name[-1])
                    if name[:3] == "pin":
                        load_job(W_IN, cols_at(g * NCOL), CD)
                    else:
                        load_job(pool_w[0, g], cols_at(0), CX)
            with sp.Fori(0, NJ) as j:
                chunk[0] = first(("gate_a", 0))
                load_job(W_IN, bass.ds(j * NCOL + C3, NCOL), CD, j, 2 * CD)
                load_job(w_pool_out[0], bass.ds(j * NCOL, NCOL), CD, j, 2 * CD)
            chunk[0] = first("C0")
            load_job(W_IN, cols_at(C1 + INNER + GROUPS * P), CD)
            load_job(W_IN, cols_at(C1 + INNER + NCOL), CD)
            load_job(W_IN, cols_at(C1 + INNER + GROUPS * P + NCOL), CD)
            with sp.Fori(0, GROUPS) as g:
                chunk[0] = first(("x", 0))
                load_job(W_IN, bass.ds(g * NCOL + C1, NCOL), CD, g, 2 * CD)
                load_job(W_IN, bass.ds(g * NCOL + D, NCOL), CD, g, 2 * CD)
            chunk[0] = first(("gate_b", 0))
            for j in range(NJ):
                load_job(W_IN, cols_at(C3 + D + j * NCOL), CD)
            with sp.Fori(0, NJ) as j:
                chunk[0] = first(("ssd_out", 0))
                load_job(w_ssd_out[0], bass.ds(j * NCOL, NCOL), CI, j, CI)
            chunk[0] = first(("mix_out", 0))
            for j in range(NJ):
                load_job(w_mix_out[0], cols_at(j * NCOL), CD)
            for w in (w_k, w_q, w_v):
                load_job(w[0], cols_at(0), CD)
            for j in range(NJ):
                load_job(w_xo[0], cols_at(j * NCOL), CX)
            ffn(1, ffn2_w1, ffn2_w3, ffn2_w2)
            assert chunk[0] == NCH
            for n in range(2 * T):
                t, c = n // 2, slice(n % 2 * D // 2, (n % 2 + 1) * D // 2)
                sp.wait_ge(res_ready, updates_before(4) + n + 1)
                sp.dma_start(out[0, t * P:(t + 1) * P, c], res[:, t, c]).then_inc(stored, 16)
            sp.wait_ge(stored, 16 * 2 * T)

        @block.gpsimd
        def _(pool):
            def load_row(name, src, i=None):
                s = slot(name)
                pool.wait_ge(evacuated[s], lin(number(name) // 2, i, 1))
                pool.dma_start(row_bc[:, s], src.to_broadcast([P, NCOL])).then_inc(row_loaded[s], 16)

            def down_rows(f, g):
                with pool.Fori(0, NJ // 2) as i:
                    for o in range(2):
                        load_row(("down", f, o), g[0:1, bass.ds(i * (2 * NCOL) + o * NCOL, NCOL)], i)

            down_rows(0, ffn1_post_g)
            pool.wait_ge(used, end(("down", 0, NJ - 1)))
            pool.dma_start(dtb_bc[:], dt_bias[0:1, :].to_broadcast([P, HEADS])).then_inc(mix_loaded, 16)
            pool.dma_start(alog_bc[:], a_log[0:1, :].to_broadcast([P, HEADS])).then_inc(mix_loaded, 16)
            pool.dma_start(upper[:], anticausal).then_inc(mix_loaded, 16)
            pool.dma_start(invc[:], inv_count.rearrange("(o w) n -> o w n", o=1).to_broadcast([P, 4, S])).then_inc(mix_loaded, 16)
            pool.wait_ge(t_moved[1], use(1, "csT"))
            pool.dma_start(cs_dram.rearrange("t h n -> (t h) n"), cst[:]).then_inc(cs_stored, 16)
            pool.wait_ge(cs_stored, 16)
            pool.wait_ge(pooled_low, len(WINDOWS))

            def load_csb(g):
                for t in range(T):
                    pool.dma_start(csb[:, :, t, :], cs_dram[t:t + 1, bass.ds(g * HPG, HPG), :].to_broadcast([P, HPG, P])).then_inc(csb_loaded, 16)

            load_csb(0)
            with pool.Fori(0, NJ) as j:
                load_row(("gate_a", 0), b_gate[0:1, bass.ds(j * NCOL, NCOL)], j)
            with pool.Fori(1, GROUPS) as g:
                pool.wait_ge(seg_ready, g)
                load_csb(g)
            for j in range(NJ):
                load_row(("gate_b", j), b_gate[0:1, D + j * NCOL:D + (j + 1) * NCOL])
            pool.wait_ge(used, end(("ssd_out", NJ - 1)))
            pool.dma_start(memx[:], mem[0].rearrange("(t p) d -> p t d", p=P)).then_inc(mem_loaded, 16)
            for j in range(NJ):
                load_row(("mix_out", j), mix_post_g[0:1, j * NCOL:(j + 1) * NCOL])
            for j in range(NJ):
                load_row(("xo", j), xattn_post_g[0:1, j * NCOL:(j + 1) * NCOL])
            down_rows(1, ffn2_post_g)

        @block.tensor
        def _(pe):
            chunk = [0]

            def take(i=None, per=0):
                c = chunk[0]
                pe.wait_ge(high, lin(c + 1, i, per))
                pe.wait_ge(low, lin(c + 1, i, per))
                chunk[0] += 1
                return c % RING

            def claim(name, i=None, per=1):
                n = number(name)
                if n >= 2:
                    pe.wait_ge(evacuated[n % 2], lin(n // 2, i, per))

            def token_chunks(name, xh, xl, ks, last_k, i=None, per=0, before=None):
                o = tok(slot(name))
                for k in ks:
                    if before is not None:
                        before(k)
                    r = take(i, per)
                    for kk in range(CK):
                        for t in range(T):
                            a, b = xh[:, k * CK + kk, t * P:(t + 1) * P], xl[:, k * CK + kk, t * P:(t + 1) * P]
                            nc.tensor.matmul(o[:, t], b, wh[:, r, kk], start=(k == 0 and kk == 0), stop=False)
                            nc.tensor.matmul(o[:, t], a, wh[:, r, kk], start=False, stop=False)
                            mm = nc.tensor.matmul(o[:, t], a, wl[:, r, kk], start=False,
                                                  stop=(k == last_k and kk == CK - 1))
                    mm.then_inc(used, 1)

            def feature_chunks(name, xh, xl, ks, last_k, i=None, per=0, before=None):
                o = feat(slot(name))
                for k in ks:
                    if before is not None:
                        before(k)
                    r = take(i, per)
                    for kk in range(CK):
                        a, b = xh[:, k * CK + kk], xl[:, k * CK + kk]
                        for m in range(M):
                            h, l = wh[:, r, kk, m * P:(m + 1) * P], wl[:, r, kk, m * P:(m + 1) * P]
                            nc.tensor.matmul(o[:, m], h, b, start=(k == 0 and kk == 0 and m % 2 == 0), stop=False,
                                             skip_group_check=True)
                            nc.tensor.matmul(o[:, m], h, a, start=False, stop=False, skip_group_check=True)
                            mm = nc.tensor.matmul(o[:, m], l, a, start=False,
                                                  stop=(k == last_k and kk == CK - 1), skip_group_check=True)
                    mm.then_inc(used, 1)

            def claim_area(k, name, i=None, per=1):
                n = use(k, name) - 1
                if n >= 1:
                    pe.wait_ge(t_moved[k], lin(n, i, per))

            def turn(k, src):
                o = area(k)
                for m in range(M):
                    for t in range(T):
                        tr = nc.tensor.transpose(o[:, m, t * P:(t + 1) * P], src[:, t, m * P:(m + 1) * P], ident[:])
                tr.then_inc(t_ready[k], 1)

            def turn_pre(n, qs):
                pe.wait_ge(normed, 1 + T * n)
                for q in qs:
                    claim_area(q % 2, (f"pre{n}", q))
                    turn(q % 2, F[:, :, q * NCOL:(q + 1) * NCOL])

            def turn_res(n, qs):
                for q in qs:
                    if n == 0:
                        pe.wait_ge(x_loaded, 16 * T)
                    else:
                        pe.wait_ge(res_ready, updates_before(n) + T * (q + 1))
                    claim_area(q % 2, (f"pre{n}", q))
                    turn(q % 2, res[:, :, q * NCOL:(q + 1) * NCOL])

            def pre_wait(n):
                def before(k):
                    if k % 2 == 0:
                        q = k // 2
                        pe.wait_ge(t_moved[q % 2], use(q % 2, (f"pre{n}", q)))
                return before

            def ffn(f):
                def turn_hidden(j, i=None):
                    pe.wait_ge(evacuated[slot(("up", f, 0))], lin(moved(("up", f, j)), i, 1))
                    claim_area(0, ("hidden", f, j), i)
                    turn(0, hid)

                def pair(i=None):
                    chunk[0] = first(("gate", f, 0))
                    claim(("gate", f, 0), i)
                    n = {0: 0, 1: 3}[f]
                    if i is None:
                        turn_res(n, (0, 1))
                    before = pre_wait(n) if i is None else None
                    token_chunks(("gate", f, 0), uh, ul, range(0, 2), CD - 1, i, 2 * CD, before)
                    if i is None:
                        turn_res(n, (2, 3))
                    token_chunks(("gate", f, 0), uh, ul, range(2, 3), CD - 1, i, 2 * CD, before)
                    if i is not None:
                        turn_hidden(0, i - 1)
                    token_chunks(("gate", f, 0), uh, ul, range(3, CD), CD - 1, i, 2 * CD, before)
                    claim(("up", f, 0), i)
                    token_chunks(("up", f, 0), uh, ul, range(CD), CD - 1, i, 2 * CD)

                pair()
                with pe.Fori(1, NP) as j:
                    pair(j)
                turn_hidden(NP - 1)
                with pe.Fori(0, NJ // 2) as i:
                    chunk[0] = first(("down", f, 0))
                    for o in range(2):
                        claim(("down", f, o), i)
                        token_chunks(("down", f, o), hidh, hidl, range(CF - 2), CF - 1, i, 2 * CF)
                        pe.wait_ge(t_moved[0], use(0, ("hidden", f, NP - 1)))
                        token_chunks(("down", f, o), hidh, hidl, range(CF - 2, CF), CF - 1, i, 2 * CF)
                chunk[0] = end(("down", f, NJ - 1))

            pe.wait_ge(consts_loaded, 48)
            pe.wait_ge(rows_loaded, 160)
            widths = (P, 96, 96, 48)
            for n, wd in enumerate(widths):
                tr = nc.tensor.transpose(J[:, 0, 0, sum(widths[:n]):sum(widths[:n + 1])], rows[0:wd, n, :], ident[0:wd, 0:wd])
            tr.then_inc(cols_ready, 1)
            pe.wait_ge(cols_ready, 2)
            ffn(0)

            claim("pin0")
            turn_pre(1, (0, 1))
            feature_chunks("pin0", uh, ul, range(0, 2), CD - 1, before=pre_wait(1))
            turn_pre(1, (2, 3))
            feature_chunks("pin0", uh, ul, range(2, CD), CD - 1, before=pre_wait(1))
            claim("dt")
            r = take()
            o = tok(slot("dt"))
            wdh = wh[:, r].rearrange("p k n -> p (k n)").rearrange("p (k n) -> p k n", n=HEADS)
            wdl = wl[:, r].rearrange("p k n -> p (k n)").rearrange("p (k n) -> p k n", n=HEADS)
            for t in range(T):
                for k in range(KD):
                    a, b = uh[:, k, t * P:(t + 1) * P], ul[:, k, t * P:(t + 1) * P]
                    nc.tensor.matmul(o[:, t, 0:HEADS], b, wdh[:, k], start=(k == 0), stop=False)
                    nc.tensor.matmul(o[:, t, 0:HEADS], a, wdh[:, k], start=False, stop=False)
                    mm = nc.tensor.matmul(o[:, t, 0:HEADS], a, wdl[:, k], start=False, stop=(k == KD - 1))
            mm.then_inc(used, 1)

            def feature_job(name, xh=uh, xl=ul, n=CD, before=None):
                claim(name)
                feature_chunks(name, xh, xl, range(n), n - 1, before=before)

            claim("pin1")
            feature_chunks("pin1", uh, ul, range(0, 6), CD - 1)
            pe.wait_ge(a_ready, 1)
            pe.wait_ge(mix_loaded, 64)
            claim_area(1, "cs")
            nc.tensor.matmul(A[:, 1, 0, 0:T * HEADS], tri[:], small[:, AV:AV + T], start=True, stop=True)
            nc.tensor.matmul(A[:, 1, 1, 0:HEADS], upper[:], small[:, AV], start=True, stop=True).then_inc(t_ready[1], 1)
            feature_chunks("pin1", uh, ul, range(6, CD), CD - 1)
            claim_area(1, "csT")
            nc.tensor.transpose(A[:, 1, 0, 0:P], small[:, CS:CS + T].rearrange("p t h -> p (t h)"), ident[:]).then_inc(t_ready[1], 1)
            for name in ("pw0", "pin2", "pw1", "pin3", "pw2", "B0", "pw3"):
                if name[:2] == "pw":
                    pe.wait_ge(pooled_low, int(name[-1]) + 1)
                    feature_job(name, poolh, pooll, CX)
                else:
                    feature_job(name)
            with pe.Fori(0, NJ) as j:
                chunk[0] = first(("gate_a", 0))
                claim(("gate_a", 0), j)
                token_chunks(("gate_a", 0), uh, ul, range(CD), CD - 1, j, 2 * CD)
                claim(("pool_out", 0), j)
                token_chunks(("pool_out", 0), mixh, mixl, range(CD), CD - 1, j, 2 * CD)
            chunk[0] = first("C0")
            feature_job("C0")

            def cb(half):
                pe.wait_ge(bc_silu, 2 * half + 2)
                for pair in range(2):
                    claim_area(1, ("cb", 2 * half + pair))
                    for q in range(2):
                        m = 2 * pair + q
                        nc.tensor.matmul(A[:, 1, q, 0:S], bT[:, m, 0:P], cT[:, m, :], start=True, stop=True)
                        mm = nc.tensor.matmul(A[:, 1, q, S:S + P], bT[:, m, P:S], cT[:, m, P:S], start=True, stop=True)
                    mm.then_inc(t_ready[1], 1)

            claim("B1")
            feature_chunks("B1", uh, ul, range(0, 5), CD - 1)
            cb(0)
            feature_chunks("B1", uh, ul, range(5, CD), CD - 1)
            feature_job("C1")

            def turn_y(g0, i=None):
                pe.wait_ge(y_normed, lin(g0 + 1, i, 1))
                claim_area(0, ("yT", g0), i, 2)
                turn(0, yb)

            def group(i=None):
                chunk[0] = first(("x", 0))
                per = 2 * CD
                claim(("x", 0), i)
                feature_chunks(("x", 0), uh, ul, range(0, 6), CD - 1, i, per)
                if i is None:
                    cb(1)
                else:
                    turn_y(0, i - 1)
                feature_chunks(("x", 0), uh, ul, range(6, CD), CD - 1, i, per)
                claim(("z", 0), i)
                token_chunks(("z", 0), uh, ul, range(0, 5), CD - 1, i, per)
                pe.wait_ge(xc_silu, lin(1, i, 1))
                claim_area(0, ("xT", 0), i, 2)
                for t in range(T):
                    for m in range(M):
                        tr = nc.tensor.transpose(A[:, 0, t, m * P:(m + 1) * P], xc[:, m, t * P:(t + 1) * P], ident[:])
                tr.then_inc(t_ready[0], 1)
                token_chunks(("z", 0), uh, ul, range(5, CD), CD - 1, i, per)
                pe.wait_ge(w_ready, lin(1, i, 1))
                pe.wait_ge(xdt_ready, lin(1, i, 1))
                claim_area(1, ("Y", 0), i)
                for h in range(HPG):
                    c = slice(h * HEAD_DIM, (h + 1) * HEAD_DIM)
                    nc.tensor.matmul(A[:, 1, 0, c], E[:, h, 0:P], Xdt[:, 0, c], start=True, stop=True)
                    nc.tensor.matmul(A[:, 1, 1, c], E[:, h, P:2 * P], Xdt[:, 0, c], start=True, stop=False)
                    mm = nc.tensor.matmul(A[:, 1, 1, c], E[:, h, 2 * P:3 * P], Xdt[:, 1, c], start=False, stop=True)
                mm.then_inc(t_ready[1], 1)

            group()
            with pe.Fori(1, GROUPS) as g:
                group(g)
            chunk[0] = first(("gate_b", 0))
            for j in range(NJ):
                claim(("gate_b", j))
                token_chunks(("gate_b", j), uh, ul, range(0, 6), CD - 1)
                if j == 0:
                    turn_y(GROUPS - 1)
                token_chunks(("gate_b", j), uh, ul, range(6, CD), CD - 1)
            pe.wait_ge(yn_low, GROUPS)

            def turn_merged(j):
                pe.wait_ge(merged, NJ + j + 1)
                claim_area(0, ("merged", j))
                turn(0, F[:, :, j * NCOL:(j + 1) * NCOL])

            for j in range(NJ):
                claim(("ssd_out", j))
                token_chunks(("ssd_out", j), ynh, ynl, range(0, 3), CI - 1)
                if j >= 1:
                    turn_merged(j - 1)
                token_chunks(("ssd_out", j), ynh, ynl, range(3, CI), CI - 1)
            for j in range(NJ):
                claim(("mix_out", j))
                if j == 0:
                    pe.wait_ge(t_moved[0], use(0, ("merged", NJ - 2)))
                for k in range(CD):
                    if j == 0 and k == 3:
                        turn_merged(NJ - 1)
                    if j == 0 and k == CD - 2:
                        pe.wait_ge(t_moved[0], use(0, ("merged", NJ - 1)))
                    if (j, k) in ((1, 3), (1, 6), (2, 1), (2, 4)):
                        q = ((1, 3), (1, 6), (2, 1), (2, 4)).index((j, k))
                        pe.wait_ge(mem_normed, T)
                        claim_area(0, ("mem", q))
                        turn(0, memx[:, :, q * NCOL:(q + 1) * NCOL])
                    token_chunks(("mix_out", j), uh, ul, range(k, k + 1), CD - 1)

            pe.wait_ge(t_moved[0], use(0, ("mem", 3)))
            claim("k")
            feature_chunks("k", memh, meml, range(0, 7), CD - 1)
            turn_pre(2, (0, 1))
            feature_chunks("k", memh, meml, range(7, CD), CD - 1)
            claim("q")
            feature_chunks("q", uh, ul, range(0, 2), CD - 1, before=pre_wait(2))
            turn_pre(2, (2, 3))
            feature_chunks("q", uh, ul, range(2, CD), CD - 1, before=pre_wait(2))
            claim("v")
            token_chunks("v", memh, meml, range(0, 1), CD - 1)
            pe.wait_ge(evacuated[slot("k")], moved("k"))
            pe.wait_ge(evacuated[slot("q")], moved("q"))
            for t in range(T):
                claim_area(t, f"score{t}")
                for h in range(X_HEADS):
                    mm = nc.tensor.matmul(area(t)[:, h], qT[:, h, t * P:(t + 1) * P], kT[:, h], start=True, stop=True)
                mm.then_inc(t_ready[t], 1)
            token_chunks("v", memh, meml, range(1, 7), CD - 1)
            pe.wait_ge(probs_scaled, T)
            for mt in range(T):
                claim_area(mt, f"probT{mt}")
                for h in range(X_HEADS):
                    for t in range(T):
                        tr = nc.tensor.transpose(area(mt)[:, h, t * P:(t + 1) * P], prob[:, t, h, mt * P:(mt + 1) * P], ident[:])
                tr.then_inc(t_ready[mt], 1)
            token_chunks("v", memh, meml, range(7, CD), CD - 1)
            claim("attend")
            pe.wait_ge(evacuated[slot("v")], moved("v"))
            for mt in range(T):
                pe.wait_ge(t_moved[mt], use(mt, f"probT{mt}"))
            for h in range(X_HEADS):
                for mt in range(T):
                    mm = nc.tensor.matmul(feat(slot("attend"))[:, h], V[:, mt, h * P:(h + 1) * P], probT[:, mt, h],
                                          start=(mt == 0), stop=(mt == T - 1), skip_group_check=True)
            mm.then_inc(o_high, 1)
            pe.wait_ge(evacuated[slot("attend")], moved("attend"))
            for j in range(NJ):
                claim(("xo", j))
                token_chunks(("xo", j), oh, ol, range(CX), CX - 1)

            ffn(1)
            assert chunk[0] == NCH

        @block.scalar
        def _(act):
            at_chunk = [0]
            for t in range(T):
                act.dma_start(res[:, t], x[0, t * P:(t + 1) * P, :]).then_inc(x_loaded, 16)

            def advance(i=None, per=0):
                c = at_chunk[0] + AHEAD
                at_chunk[0] += 1
                if c < NCH:
                    r = c % RING
                    act.wait_ge(loaded[r], lin(16 * (c // RING + 1), i, 16 * per // RING))
                    if i is not None or c >= RING:
                        act.wait_ge(used, lin(c - RING + 1, i, per))
                    nc.scalar.activation(wh[:, r], raw[:, r], ACT.Copy).then_inc(high, 1)

            def to(n, i=None, per=0):
                assert at_chunk[0] <= n, (at_chunk[0], n)
                while at_chunk[0] < n:
                    advance(i, per)

            def done(i=None, per=0):
                act.wait_ge(used, lin(at_chunk[0], i, per))

            for r in range(AHEAD):
                act.wait_ge(loaded[r], 16)
                nc.scalar.activation(wh[:, r], raw[:, r], ACT.Copy).then_inc(high, 1)

            roots = [0]

            def root(n, i=None, ap=slice(0, T)):
                act.wait_ge(var_ready, lin(n, i, 1))
                nc.scalar.activation(ss[:, ap], sv[:, ap], ACT.Sqrt).then_inc(root_ready, 1)

            def next_root(ap=slice(0, T)):
                roots[0] += 1
                root(roots[0], None, ap)

            def job_square(name, n, i=None, col=None):
                if not (isinstance(n, int) and n == 0):
                    act.wait_ge(job_squares, n if isinstance(n, int) else n)
                for t in range(T):
                    sq = nc.scalar.activation(A[:, 1, t], tok(slot(name))[:, t], ACT.Square,
                                              accum_out=ssq_job[:, t, col])
                sq.then_inc(job_squares, 1)

            def split_area(k, name, gain, dst, i=None, per=1, iper=1):
                act.wait_ge(t_ready[k], lin(use(k, name), i, iper))
                for m in range(M):
                    a = nc.scalar.activation(dst[:, m], area(k)[:, m], ACT.Copy, scale=cols[:, gain + m:gain + m + 1])
                a.then_inc(t_high[k], 1)

            def pre_high(n, q):
                split_area(q % 2, (f"pre{n}", q), G_COL[f"pre{n}"] + q * M, uh[:, q * M:(q + 1) * M])

            def res_square(n, t):
                if n == 0:
                    act.wait_ge(x_loaded, 16 * T)
                elif UPDATES[n] == T:
                    act.wait_ge(res_ready, updates_before(n) + t + 1)
                else:
                    act.wait_ge(res_ready, updates_before(n + 1))
                nc.scalar.activation(F[:, t], res[:, t], ACT.Square, accum_out=ssq_res[:, t:t + 1]).then_inc(res_squares, 1)

            def pre_norm(n):
                for t in range(T):
                    res_square(n, t)
                for t in range(T):
                    next_root(slice(t, t + 1))
                for q in range(4):
                    pre_high(n, q)

            def pre_norm_behind(n):
                pre_high(n, 0)
                pre_high(n, 1)
                for t in range(T):
                    res_square(n, t)
                pre_high(n, 2)
                pre_high(n, 3)
                next_root()

            def ffn(f):
                def silu(i=None):
                    done(i, 2 * CD)
                    if i is not None:
                        act.wait_ge(evacuated[slot(("up", f, 0))], lin(moved(("up", f, 0)), i - 1, 1))
                    if i is None:
                        act.wait_ge(normed, {0: 1, 1: 2 * T + 2}[f])
                    for t in range(T):
                        a = nc.scalar.activation(silu_g[:, t], tok(slot(("gate", f, 0)))[:, t], ACT.Silu, scale=sr_ffn[:, t:t + 1])
                    a.then_inc(evacuated[slot(("gate", f, 0))], 1)

                def hidden_high(i=None, j=0):
                    act.wait_ge(t_ready[0], lin(use(0, ("hidden", f, j)), i, 1))
                    dst = hidh[:, j * M:(j + 1) * M] if i is None else hidh[:, bass.ds(i * M, M)]
                    nc.scalar.activation(dst, area(0), ACT.Copy).then_inc(t_high[0], 1)

                c0 = first(("gate", f, 0))

                def pair(i=None):
                    at_chunk[0] = c0
                    to(c0 + 3, i, 2 * CD)
                    if i is not None:
                        hidden_high(i - 1)
                    to(c0 + CD, i, 2 * CD)
                    silu(i)
                    to(c0 + 2 * CD, i, 2 * CD)

                pair()
                with act.Fori(1, NP) as j:
                    pair(j)
                at_chunk[0] = first(("down", f, 0))
                hidden_high(None, NP - 1)
                base = {0: 0, 1: 3 * NJ}[f]
                d0 = first(("down", f, 0))

                if f == 0:
                    with act.Fori(0, NJ // 2) as i:
                        at_chunk[0] = d0
                        for o in range(2):
                            to(d0 + (o + 1) * CF, i, 2 * CF)
                            done(i, 2 * CF)
                            before = names[number(("down", f, o)) - 1]
                            act.wait_ge(evacuated[slot(before)], i + moved(before))
                            for t in range(T):
                                sq = nc.scalar.activation(A[:, 1, t], tok(slot(("down", f, o)))[:, t], ACT.Square,
                                                          accum_out=ssq_job[:, t, bass.ds(i * 2 + o, 1)])
                            sq.then_inc(job_squares, 1)
                    at_chunk[0] = end(("down", f, NJ - 1))
                else:
                    for j in range(NJ):
                        to(end(("down", f, j)))
                        done()
                        job_square(("down", f, j), base + j, col=slice(j, j + 1))

            act.wait_ge(cols_ready, 2)
            pre_norm_behind(0)
            ffn(0)
            next_root()
            pre_norm(1)
            to(end("pin0"))
            done()
            nc.scalar.activation(pool_x[:], feat(slot("pin0")), ACT.Copy).then_inc(evacuated[slot("pin0")], 1)

            to(end("dt") + 1)
            act.wait_ge(mix_loaded, 64)
            nc.scalar.activation(small[:, EA], alog_bc[:], ACT.Exp).then_inc(dt_func, 1)
            act.wait_ge(evacuated[slot("dt")], moved("dt"))
            nc.scalar.activation(small[:, EX:EX + T], small[:, DTR:DTR + T], ACT.Abs).then_inc(dt_func, 1)
            act.wait_ge(dt_func, 2)
            nc.scalar.activation(small[:, EX:EX + T], small[:, EX:EX + T], ACT.Exp, scale=-1.0).then_inc(dt_func, 1)
            to(end("dt") + 2)
            act.wait_ge(dt_step, 1)
            nc.scalar.activation(small[:, LG:LG + T], small[:, AB:AB + T], ACT.Ln).then_inc(dt_func, 1)

            def pool_in(g):
                to(end(f"pin{g}"))
                done()
                act.wait_ge(pooled_ready, g)
                nc.scalar.activation(pool_x[:], feat(slot(f"pin{g}")), ACT.Copy).then_inc(evacuated[slot(f"pin{g}")], 1)

            def pool_high(g):
                act.wait_ge(pooled_ready, g + 1)
                if g >= 1:
                    act.wait_ge(used, end(f"pw{g - 1}"))
                nc.scalar.activation(poolh[:], win_a[:], ACT.Copy).then_inc(pooled_high, 1)

            def pool_mixed(g):
                to(end(f"pw{g}"))
                done()
                for m in range(M):
                    c = PS_COL + g * M + m
                    a = nc.scalar.activation(mixh[:, g * M + m], feat(slot(f"pw{g}"))[:, m], ACT.Copy, scale=cols[:, c:c + 1])
                a.then_inc(pw_high, 1)

            to(end("dt") + 3)
            pool_high(0)
            pool_in(1)
            pool_mixed(0)
            to(end("pw0") + 3)
            pool_high(1)
            pool_in(2)
            pool_mixed(1)
            to(end("pw1") + 3)
            pool_high(2)
            pool_in(3)
            pool_mixed(2)
            to(end("pw2") + 3)
            pool_high(3)

            def conv_silu(name, dst, n, i=None, per=0):
                act.wait_ge(evacuated[slot(name)], lin(moved(name), i, 1))
                nc.scalar.activation(dst, dst, ACT.Silu).then_inc(n, 1)

            pool_mixed(3)
            c0 = first(("gate_a", 0))
            with act.Fori(0, NJ) as j:
                at_chunk[0] = c0
                to(c0 + CD + 1, j, 2 * CD)
                act.wait_ge(gate_biased, j + 1)
                nc.scalar.activation(sig_a[:], sig_a[:], ACT.Sigmoid).then_inc(gate_ready, 1)
                to(c0 + 2 * CD, j, 2 * CD)
            at_chunk[0] = first("C0")
            conv_silu("B0", bT[:], bc_silu)
            to(end("C0") + 4)
            conv_silu("C0", cT[:], bc_silu)
            to(end("B1") + 4)
            conv_silu("B1", bT[:], bc_silu)
            to(end("C1"))

            def finish_square(g0, i=None):
                act.wait_ge(gated, lin(g0 + 1, i, 1))
                for t in range(T):
                    sq = nc.scalar.activation(zs[:, t], yb[:, t], ACT.Square, accum_out=ssq_res[:, t:t + 1])
                sq.then_inc(y_squares, 1)

            def finish_z(g0, i=None):
                act.wait_ge(used, lin(end(("z", g0)), i, 2 * CD))
                if i is not None or g0 >= 1:
                    act.wait_ge(root_ready, lin(g_root + g0, i, 1))
                nc.scalar.activation(zs[:], tok(slot(("z", 0))), ACT.Silu).then_inc(evacuated[slot(("z", 0))], 1)

            def finish_y(g0, i=None):
                act.wait_ge(t_ready[0], lin(use(0, ("yT", g0)), i, 2))
                for m in range(M):
                    if i is None:
                        dst, sc = yn[:, g0 * M + m], cols[:, NG_COL + g0 * M + m:NG_COL + g0 * M + m + 1]
                    else:
                        dst = yn[:, bass.ds(i * M + (g0 * M + m), 1)].rearrange("p a n -> p (a n)")
                        sc = cols[:, bass.ds(i * M + (NG_COL + g0 * M + m), 1)]
                    a = nc.scalar.activation(dst, area(0)[:, m], ACT.Copy, scale=sc)
                a.then_inc(t_moved[0], 1)

            g_root = roots[0]

            def group(i=None):
                c0 = first(("x", 0))
                at_chunk[0] = c0
                per = 2 * CD
                if i is not None:
                    finish_z(0, i - 1)
                to(c0 + 2, i, per)
                if i is not None:
                    finish_square(0, i - 1)
                to(c0 + 3, i, per)
                if i is not None:
                    root(g_root + 1, i - 1)
                else:
                    to(c0 + 4)
                    conv_silu("C1", cT[:], bc_silu)
                to(c0 + 7, i, per)
                if i is not None:
                    finish_y(0, i - 1)
                to(c0 + CD, i, per)
                act.wait_ge(seg_ready, lin(1, i, 1))
                nc.scalar.activation(E[:], E[:], ACT.Exp).then_inc(exp_ready, 1)
                to(c0 + CD + 4, i, per)
                conv_silu(("x", 0), xc[:], xc_silu, i)
                to(c0 + CD + 6, i, per)
                act.wait_ge(t_ready[0], lin(use(0, ("xT", 0)), i, 2))
                if i is not None:
                    act.wait_ge(gated, i)
                nc.scalar.activation(X[:], A[:, 0], ACT.Copy).then_inc(t_moved[0], 1)
                to(c0 + 2 * CD, i, per)

            group()
            with act.Fori(1, GROUPS) as g:
                group(g)
            c0 = first(("gate_b", 0))
            at_chunk[0] = c0
            finish_z(GROUPS - 1)
            to(c0 + 2)
            finish_square(GROUPS - 1)
            to(c0 + 3)
            roots[0] = g_root + GROUPS
            root(roots[0])
            to(c0 + 7)
            finish_y(GROUPS - 1)

            def yn_split(b):
                act.wait_ge(t_moved[0], use(0, ("yT", GROUPS - 1)))
                nc.scalar.activation(ynh[:, b * M:(b + 1) * M], yn[:, b * M:(b + 1) * M], ACT.Copy).then_inc(yn_high, 1)

            for j in range(NJ):
                to(end(("gate_b", j)) + 1)
                act.wait_ge(gate_biased, NJ + j + 1)
                nc.scalar.activation(sig_b[:, :, j * NCOL:(j + 1) * NCOL], sig_b[:, :, j * NCOL:(j + 1) * NCOL],
                                     ACT.Sigmoid).then_inc(gate_ready, 1)
                if j < NJ - 1:
                    for b in range(3 * j, min(3 * j + 3, GROUPS)):
                        to(end(("gate_b", j)) + 2 + b - 3 * j)
                        yn_split(b)
            for j in range(NJ):
                nxt = first(("ssd_out", j + 1)) if j < NJ - 1 else first(("mix_out", 0))
                to(nxt + 3)
                act.wait_ge(t_ready[0], use(0, ("merged", j)))
                nc.scalar.activation(uh[:, j * M:(j + 1) * M], area(0), ACT.Copy).then_inc(t_high[0], 1)
            to(first(("mix_out", 0)) + 4)
            act.wait_ge(mem_loaded, 16)
            for t in range(T):
                if t >= 1:
                    act.wait_ge(mem_squares, t)
                nc.scalar.activation(mem_junk[:], memx[:, t], ACT.Square, accum_out=ssq_res[:, t:t + 1]).then_inc(mem_squares, 1)
                to(at_chunk[0] + 1)
            next_root()
            for j in range(NJ):
                to(end(("mix_out", j)))
                done()
                job_square(("mix_out", j), NJ + j, col=slice(j, j + 1))
                marks = {0: ((1, 3, 0), (1, 6, 1)), 1: ((2, 1, 2), (2, 4, 3))}.get(j, ())
                for jj, k, q in marks:
                    to(first(("mix_out", jj)) + k)
                    split_area(0, ("mem", q), G_COL["mem"] + q * M, memh[:, q * M:(q + 1) * M])

            next_root()

            advance()
            res_square(2, 0)
            advance()
            res_square(2, 1)
            advance()
            for t in range(T):
                next_root(slice(t, t + 1))
                advance()
            to(first("k") + 7)
            pre_high(2, 0)
            pre_high(2, 1)
            to(end("k"))
            done()
            nc.scalar.activation(kT[:], feat(slot("k")), ACT.Copy).then_inc(evacuated[slot("k")], 1)
            to(end("k") + 2)
            pre_high(2, 2)
            pre_high(2, 3)
            to(end("q"))
            done()
            nc.scalar.activation(qT[:], feat(slot("q")), ACT.Copy).then_inc(evacuated[slot("q")], 1)
            to(first("v") + 2)
            scale = float(P) ** -0.5
            for t in range(T):
                act.wait_ge(max_ready, t + 1)
                for h in range(X_HEADS):
                    n = t * X_HEADS + h
                    e = nc.scalar.activation(prob[:, t, h], area(t)[:, h], ACT.Exp, bias=smax[:, 1, n:n + 1], scale=scale,
                                             accum_out=smax[:, 2, n:n + 1])
                e.then_inc(probs, 1)
                advance()
            to(first("v") + 7)
            for mt in range(T):
                act.wait_ge(t_ready[mt], use(mt, f"probT{mt}"))
                nc.scalar.activation(probT[:, mt], area(mt), ACT.Copy).then_inc(t_moved[mt], 1)
            to(end("v"))
            done()
            nc.scalar.activation(V[:], tok(slot("v")), ACT.Copy).then_inc(evacuated[slot("v")], 1)
            act.wait_ge(o_high, 1)
            nc.scalar.activation(oh[:], feat(slot("attend")), ACT.Copy).then_inc(o_high, 1)
            for j in range(NJ):
                to(end(("xo", j)))
                done()
                job_square(("xo", j), 2 * NJ + j, col=slice(j, j + 1))
            next_root()
            pre_norm_behind(3)
            ffn(1)
            next_root()

        @block.vector
        def _(dve):
            at_chunk = [0]
            steps = [0]
            loop = [None, 0]

            def link(ins):
                steps[0] += 1
                ins.then_inc(step, 1)
                dve.wait_ge(step, lin(steps[0], *loop))

            def advance(i=None, per=0):
                c = at_chunk[0] + AHEAD
                at_chunk[0] += 1
                if c < NCH:
                    r = c % RING
                    dve.wait_ge(high, lin(c + 1, i, per))
                    nc.vector.tensor_tensor(wl[:, r], raw[:, r], wh[:, r].bitcast(F32), ALU.subtract).then_inc(low, 1)

            def to(n, i=None, per=0):
                assert at_chunk[0] <= n, (at_chunk[0], n)
                while at_chunk[0] < n:
                    advance(i, per)

            def done(i=None, per=0):
                dve.wait_ge(used, lin(at_chunk[0], i, per))

            for r in range(AHEAD):
                dve.wait_ge(high, r + 1)
                nc.vector.tensor_tensor(wl[:, r], raw[:, r], wh[:, r].bitcast(F32), ALU.subtract).then_inc(low, 1)

            roots = [0]

            def inv_root(total, n_elem, i=None, base=None, ap=slice(0, T), factor=None):
                if base is None:
                    roots[0] += 1
                    base = roots[0]
                nc.vector.tensor_scalar(sv[:, ap], total, 1.0 / n_elem, EPS, ALU.mult, ALU.add).then_inc(var_ready, 1)
                dve.wait_ge(root_ready, lin(base, i, 1))
                link(nc.vector.reciprocal(sr[:, ap], ss[:, ap]))
                if factor is not None:
                    link(nc.vector.tensor_scalar(sr[:, ap], sr[:, ap], factor, None, ALU.mult))

            def row_wait(name, i=None):
                dve.wait_ge(row_loaded[slot(name)], lin(16 * row_count(name), i, 16))

            def gained(name, n, i=None, col=None):
                dve.wait_ge(job_squares, n)
                row_wait(name, i)
                nc.vector.tensor_tensor(F[:, :, col], tok(slot(name)),
                                        row_bc[:, slot(name)].unsqueeze(1).to_broadcast([P, T, NCOL]),
                                        ALU.mult).then_inc(evacuated[slot(name)], 1)

            def update(n, t, c):
                nc.vector.scalar_tensor_tensor(out=res[:, t, c], in0=F[:, t, c], scalar=sr[:, t:t + 1], in1=res[:, t, c],
                                               op0=ALU.mult, op1=ALU.add).then_inc(res_ready, 1)

            def post_norm(n, last_name, factor=None, pause=lambda: None):
                dve.wait_ge(evacuated[slot(last_name)], moved(last_name))
                link(nc.vector.tensor_reduce(ssum, ssq_job, AX.X, ALU.add))
                inv_root(ssum, D, factor=factor)
                pause()
                if UPDATES[n] == T:
                    for t in range(T):
                        update(n, t, slice(0, D))
                        pause()
                elif UPDATES[n] == NJ * T:
                    for q in range(NJ):
                        for t in range(T):
                            update(n, t, slice(q * NCOL, (q + 1) * NCOL))
                else:
                    for t in range(T):
                        for q in range(2):
                            update(n, t, slice(q * D // 2, (q + 1) * D // 2))

            def low_area(k, name, gain, hi, dst, i=None):
                dve.wait_ge(t_high[k], high_use(k, name))
                for m in range(M):
                    l = nc.vector.scalar_tensor_tensor(out=dst[:, m], in0=area(k)[:, m], scalar=cols[:, gain + m:gain + m + 1],
                                                       in1=hi[:, m].bitcast(F32), op0=ALU.mult, op1=ALU.subtract)
                l.then_inc(t_moved[k], 1)

            def pre_low(n, q):
                low_area(q % 2, (f"pre{n}", q), G_COL[f"pre{n}"] + q * M, uh[:, q * M:(q + 1) * M], ul[:, q * M:(q + 1) * M])

            def pre_scale(n, pause=lambda: None):
                for t in range(T):
                    dve.wait_ge(res_squares, T * n + t + 1)
                    inv_root(ssq_res[:, t:t + 1], D, ap=slice(t, t + 1))
                    nc.vector.tensor_scalar(F[:, t], res[:, t], sr[:, t:t + 1], None, ALU.mult).then_inc(normed, 1)
                    pause()

            def pre_norm(n):
                pre_scale(n)
                for q in range(4):
                    pre_low(n, q)

            def pre_norm_behind(n):
                for q in range(4):
                    pre_low(n, q)
                dve.wait_ge(res_squares, T * (n + 1))
                roots[0] += 1
                nc.vector.tensor_scalar(sv, ssq_res, 1.0 / D, EPS, ALU.mult, ALU.add).then_inc(var_ready, 1)
                dve.wait_ge(root_ready, roots[0])
                nc.vector.reciprocal(sr_ffn, ss).then_inc(normed, 1)

            def ffn(f):
                c0 = first(("gate", f, 0))
                g, u = ("gate", f, 0), ("up", f, 0)

                def hidden_low(i=None, j=0):
                    dve.wait_ge(t_high[0], lin(high_use(0, ("hidden", f, j)), i, 1))
                    sl = slice(j * M, (j + 1) * M) if i is None else bass.ds(i * M, M)
                    nc.vector.tensor_tensor(hidl[:, sl], area(0), hidh[:, sl].bitcast(F32), ALU.subtract).then_inc(t_moved[0], 1)

                def pair(i=None):
                    at_chunk[0] = c0
                    to(c0 + 3, i, 2 * CD)
                    if i is not None:
                        hidden_low(i - 1)
                    to(c0 + 2 * CD, i, 2 * CD)
                    done(i, 2 * CD)
                    dve.wait_ge(evacuated[slot(g)], lin(moved(g), i, 1))
                    for t in range(T):
                        h = nc.vector.scalar_tensor_tensor(out=hid[:, t], in0=tok(slot(u))[:, t], scalar=sr_ffn[:, t:t + 1],
                                                           in1=silu_g[:, t], op0=ALU.mult, op1=ALU.mult)
                    h.then_inc(evacuated[slot(u)], 1)

                pair()
                with dve.Fori(1, NP) as j:
                    pair(j)
                at_chunk[0] = first(("down", f, 0))
                hidden_low(None, NP - 1)
                d0 = first(("down", f, 0))
                if f == 0:
                    with dve.Fori(0, NJ // 2) as i:
                        at_chunk[0] = d0
                        for o in range(2):
                            to(d0 + (o + 1) * CF, i, 2 * CF)
                            gained(("down", f, o), i * 2 + (o + 1), i, bass.ds(i * (2 * NCOL) + o * NCOL, NCOL))
                    at_chunk[0] = end(("down", f, NJ - 1))
                else:
                    for j in range(NJ):
                        to(end(("down", f, j)))
                        gained(("down", f, j), 3 * NJ + j + 1, col=slice(j * NCOL, (j + 1) * NCOL))

            dve.wait_ge(cols_ready, 1)
            nc.vector.tensor_copy(cols[:], J[:, 0, 0, 0:368]).then_inc(cols_ready, 1)
            pre_norm_behind(0)
            ffn(0)
            post_norm(1, ("down", 0, NJ - 1), 0.5)
            pre_norm(1)

            def pool_window(g):
                dve.wait_ge(evacuated[slot(f"pin{g}")], moved(f"pin{g}"))
                if g >= 1:
                    dve.wait_ge(pooled_high, g)
                dve.wait_ge(step, steps[0])
                src = pool_x
                for n in range(g + 1):
                    dst = (win_a, win_b)[n % 2]
                    sh = 1 << n
                    nc.vector.tensor_copy(dst[:, :, 0:sh], src[:, :, 0:sh])
                    link(nc.vector.tensor_tensor(dst[:, :, sh:S], src[:, :, sh:S], src[:, :, 0:S - sh], ALU.add))
                    src = dst
                    if n == 1:
                        advance()
                link(nc.vector.tensor_tensor(win_b[:], src[:], invc[:, g].unsqueeze(1).to_broadcast([P, M, S]), ALU.mult))
                nc.vector.tensor_tensor(win_a[:], win_b[:], pool_x[:], ALU.subtract).then_inc(pooled_ready, 1)

            def pool_low(g):
                dve.wait_ge(pooled_high, g + 1)
                nc.vector.tensor_tensor(pooll[:], win_a[:], poolh[:].bitcast(F32), ALU.subtract).then_inc(pooled_low, 1)

            def pool_mixed(g):
                to(end(f"pw{g}"))
                dve.wait_ge(pw_high, g + 1)
                for m in range(M):
                    c = PS_COL + g * M + m
                    l = nc.vector.scalar_tensor_tensor(out=mixl[:, g * M + m], in0=feat(slot(f"pw{g}"))[:, m],
                                                       scalar=cols[:, c:c + 1], in1=mixh[:, g * M + m].bitcast(F32),
                                                       op0=ALU.mult, op1=ALU.subtract)
                l.then_inc(evacuated[slot(f"pw{g}")], 1)

            def conv(name, dst, blk, i=None, per=0, blk_per=0, pause=True):
                done(i, per)
                nb = CONV // P
                o = feat(slot(name))

                def col(tap, m):
                    c = CW_COL + tap * nb + blk + m if tap is not None else CB_COL + blk + m
                    return cols[:, c:c + 1] if i is None else cols[:, bass.ds(i * blk_per + c, 1)]

                for m in range(M):
                    l = nc.vector.tensor_scalar(dst[:, m], o[:, m], col(TAPS - 1, m), col(None, m), ALU.mult, ALU.add)
                link(l)
                for sh in range(1, TAPS):
                    for m in range(M):
                        l = nc.vector.scalar_tensor_tensor(out=dst[:, m, sh:S], in0=o[:, m, 0:S - sh], scalar=col(TAPS - 1 - sh, m),
                                                           in1=dst[:, m, sh:S], op0=ALU.mult, op1=ALU.add)
                    if sh < TAPS - 1:
                        link(l)
                    else:
                        l.then_inc(evacuated[slot(name)], 1)
                    if pause:
                        advance(i, per)

            to(end("pin0"))
            dve.wait_ge(mix_loaded, 64)
            pool_window(0)
            to(end("dt") + 1)
            dve.wait_ge(mix_loaded, 64)
            dtr, ab, ex, lg, dtv, av = (small[:, n:n + T] for n in (DTR, AB, EX, LG, DTV, AV))
            nc.vector.tensor_tensor(dtr, tok(slot("dt"))[:, :, 0:HEADS], dtb_bc[:].unsqueeze(1).to_broadcast([P, T, HEADS]),
                                    ALU.add).then_inc(evacuated[slot("dt")], 1)
            to(end("dt") + 2)
            dve.wait_ge(dt_func, 3)
            nc.vector.tensor_scalar(ab, ex, 1.0, None, ALU.add).then_inc(dt_step, 1)
            dve.wait_ge(dt_step, 1)
            dve.wait_ge(dt_func, 4)
            link(nc.vector.tensor_scalar(ab, ab, -1.0, None, ALU.add))
            link(nc.vector.tensor_scalar(dtv, ab, 1e-7, None, ALU.max))
            link(nc.vector.reciprocal(dtv, dtv))
            link(nc.vector.tensor_tensor(lg, lg, ex, ALU.mult))
            link(nc.vector.tensor_tensor(lg, lg, dtv, ALU.mult))
            link(nc.vector.scalar_tensor_tensor(out=dtv, in0=ab, scalar=0.0, in1=ex, op0=ALU.is_equal, op1=ALU.mult))
            link(nc.vector.tensor_tensor(lg, lg, dtv, ALU.add))
            link(nc.vector.scalar_tensor_tensor(out=dtv, in0=dtr, scalar=0.0, in1=lg, op0=ALU.max, op1=ALU.add))
            nc.vector.scalar_tensor_tensor(out=av, in0=dtv, scalar=-1.0, in1=small[:, EA].unsqueeze(1).to_broadcast([P, T, HEADS]),
                                           op0=ALU.mult, op1=ALU.mult).then_inc(a_ready, 1)
            to(end("dt") + 3)
            pool_low(0)
            to(first("pin1") + 6)
            dve.wait_ge(t_ready[1], use(1, "cs"))
            link(nc.vector.tensor_copy(small[:, REM], A[:, 1, 1, 0:HEADS]))
            nc.vector.tensor_copy(small[:, CS:CS + T], A[:, 1, 0, 0:T * HEADS].rearrange("p (t h) -> p t h", t=T)).then_inc(t_moved[1], 1)

            to(end("pin1"))
            pool_window(1)
            dve.wait_ge(t_ready[1], use(1, "csT"))
            nc.vector.tensor_copy(cst[:], A[:, 1, 0, 0:P]).then_inc(t_moved[1], 1)
            pool_mixed(0)
            to(end("pw0") + 3)
            pool_low(1)
            to(end("pin2"))
            pool_window(2)
            pool_mixed(1)
            to(end("pw1") + 3)
            pool_low(2)
            to(end("pin3"))
            pool_window(3)
            pool_mixed(2)
            to(end("pw2") + 3)
            pool_low(3)
            to(end("B0"))
            conv("B0", bT, INNER // P, pause=False)
            pool_mixed(3)
            c0 = first(("gate_a", 0))
            with dve.Fori(0, NJ) as j:
                at_chunk[0] = c0
                loop[0] = j
                loop[1] = 0
                to(c0 + CD, j, 2 * CD)
                done(j, 2 * CD)
                row_wait(("gate_a", 0), j)
                nc.vector.tensor_tensor(sig_a[:], tok(slot(("gate_a", 0))),
                                        row_bc[:, slot(("gate_a", 0))].unsqueeze(1).to_broadcast([P, T, NCOL]),
                                        ALU.add).then_inc(gate_biased, 1)
                dve.wait_ge(gate_biased, j + 1)
                dve.sem_inc(evacuated[slot(("gate_a", 0))], 1)
                to(c0 + 2 * CD, j, 2 * CD)
                done(j, 2 * CD)
                dve.wait_ge(gate_ready, j + 1)
                nc.vector.tensor_tensor(F[:, :, bass.ds(j * NCOL, NCOL)], tok(slot(("pool_out", 0))), sig_a[:],
                                        ALU.mult).then_inc(merged, 1)
                dve.wait_ge(merged, j + 1)
                dve.sem_inc(evacuated[slot(("pool_out", 0))], 1)
            loop[0] = None
            at_chunk[0] = first("C0")
            to(end("C0"))
            conv("C0", cT, INNER // P + GROUPS)

            def cb_masked(half):
                for pair in range(2):
                    dve.wait_ge(t_ready[1], use(1, ("cb", 2 * half + pair)))
                    for q in range(2):
                        g = 4 * half + 2 * pair + q
                        nc.vector.tensor_tensor(cbm[:, g, 0:P], A[:, 1, q, 0:P], tri[:], ALU.mult)
                        nc.vector.tensor_copy(cbm[:, g, P:2 * P], A[:, 1, q, P:2 * P])
                        l = nc.vector.tensor_tensor(cbm[:, g, 2 * P:3 * P], A[:, 1, q, 2 * P:3 * P], tri[:], ALU.mult)
                    l.then_inc(t_moved[1], 1)

            to(first("B1") + 5)
            cb_masked(0)
            to(end("B1"))
            conv("B1", bT, INNER // P + M)
            to(end("C1"))

            def heads(ap):
                return ap.rearrange("p t (h e) -> p t h e", h=HPG)

            def finish_gate(g0, i=None):
                dve.wait_ge(t_ready[1], lin(use(1, ("Y", g0)), i, 1))
                nc.vector.tensor_tensor(yb[:], A[:, 1], yb[:], ALU.add).then_inc(t_moved[1], 1)
                dve.wait_ge(t_moved[1], lin(use(1, ("Y", g0)), i, 1))
                dve.wait_ge(evacuated[slot(("z", 0))], lin(moved(("z", g0)), i, 1))
                nc.vector.tensor_tensor(yb[:], yb[:], zs[:], ALU.mult).then_inc(gated, 1)

            def finish_var(g0, i=None):
                dve.wait_ge(y_squares, lin(g0 + 1, i, 1))
                nc.vector.tensor_scalar(sv, ssq_res, 1.0 / WG, EPS, ALU.mult, ALU.add).then_inc(var_ready, 1)

            def finish_scale(g0, i=None):
                dve.wait_ge(root_ready, lin(g_root + g0 + 1, i, 1))
                link(nc.vector.reciprocal(sr, ss))
                for t in range(T):
                    l = nc.vector.tensor_scalar(yb[:, t], yb[:, t], sr[:, t:t + 1], None, ALU.mult)
                l.then_inc(y_normed, 1)

            g_root = roots[0]
            GROUP_STEPS = 5
            step0 = steps[0]

            def group(i=None):
                c0 = first(("x", 0))
                at_chunk[0] = c0
                per = 2 * CD
                steps[0] = step0 if i is None else step0 + 2
                loop[0], loop[1] = i, GROUP_STEPS
                if i is None:
                    dve.wait_ge(used, c0)
                    dve.wait_ge(t_moved[1], use(1, ("cb", 1)))
                    conv("C1", cT, INNER // P + GROUPS + M)
                else:
                    to(c0 + 1, i, per)
                    finish_gate(0, i - 1)
                    to(c0 + 3, i, per)
                    finish_var(0, i - 1)
                    to(c0 + 4, i, per)
                    finish_scale(0, i - 1)
                to(c0 + 7, i, per)
                if i is None:
                    cb_masked(1)
                    dve.wait_ge(t_moved[1], use(1, ("cb", 3)))
                dve.wait_ge(csb_loaded, lin(16 * T, i, 16 * T))
                for h in range(HPG):
                    def scalar(row):
                        return small[:, row, h:h + 1] if i is None else small[:, row, bass.ds(i * HPG + h, 1)]
                    nc.vector.tensor_scalar(E[:, h, 0:P], csb[:, h, 0], scalar(CS), 0.0, ALU.subtract, ALU.min)
                    nc.vector.tensor_scalar(E[:, h, P:2 * P], csb[:, h, 1], scalar(REM), 0.0, ALU.add, ALU.min)
                    l = nc.vector.tensor_scalar(E[:, h, 2 * P:3 * P], csb[:, h, 1], scalar(CS + 1), 0.0, ALU.subtract, ALU.min)
                l.then_inc(seg_ready, 1)
                to(c0 + CD, i, per)
                conv(("x", 0), xc, 0, i, per, M)
                to(c0 + CD + 4, i, per)
                dve.wait_ge(exp_ready, lin(1, i, 1))
                c = cbm[:, 0:1] if i is None else cbm[:, bass.ds(i, 1)]
                nc.vector.tensor_tensor(E[:], E[:], c.to_broadcast([P, HPG, 3 * P]), ALU.mult).then_inc(w_ready, 1)
                to(c0 + CD + 6, i, per)
                dve.wait_ge(t_moved[0], lin(use(0, ("xT", 0)), i, 2))
                dt_sl = slice(0, HPG) if i is None else bass.ds(i * HPG, HPG)
                nc.vector.tensor_tensor(heads(Xdt[:]), heads(X[:]), small[:, DTV:DTV + T, dt_sl].unsqueeze(3).to_broadcast([P, T, HPG, HEAD_DIM]),
                                        ALU.mult).then_inc(xdt_ready, 1)
                link(nc.vector.tensor_tensor(heads(yb[:]), heads(X[:]),
                                             d_bc[:, dt_sl].unsqueeze(1).unsqueeze(3).to_broadcast([P, T, HPG, HEAD_DIM]), ALU.mult))
                to(c0 + 2 * CD, i, per)

            group()
            assert steps[0] == step0 + GROUP_STEPS + 2, steps[0] - step0
            with dve.Fori(1, GROUPS) as g:
                group(g)
            assert steps[0] == step0 + 2 + GROUP_STEPS
            steps[0] = step0 + 2 + GROUP_STEPS * GROUPS
            loop[0] = None
            roots[0] = g_root + GROUPS
            c0 = first(("gate_b", 0))
            at_chunk[0] = c0
            to(c0 + 1)
            finish_gate(GROUPS - 1)
            to(c0 + 3)
            finish_var(GROUPS - 1)
            to(c0 + 4)
            finish_scale(GROUPS - 1)

            def yn_split(b):
                dve.wait_ge(yn_high, b + 1)
                nc.vector.tensor_tensor(ynl[:, b * M:(b + 1) * M], yn[:, b * M:(b + 1) * M],
                                        ynh[:, b * M:(b + 1) * M].bitcast(F32), ALU.subtract).then_inc(yn_low, 1)

            for j in range(NJ):
                name = ("gate_b", j)
                to(end(name))
                done()
                row_wait(name)
                nc.vector.tensor_tensor(sig_b[:, :, j * NCOL:(j + 1) * NCOL], tok(slot(name)),
                                        row_bc[:, slot(name)].unsqueeze(1).to_broadcast([P, T, NCOL]), ALU.add).then_inc(gate_biased, 1)
                dve.wait_ge(gate_biased, NJ + j + 1)
                dve.sem_inc(evacuated[slot(name)], 1)
                if j < NJ - 1:
                    for b in range(3 * j, min(3 * j + 3, GROUPS)):
                        to(end(name) + 2 + b - 3 * j)
                        yn_split(b)
            def merged_low(j):
                dve.wait_ge(t_high[0], high_use(0, ("merged", j)))
                nc.vector.tensor_tensor(ul[:, j * M:(j + 1) * M], area(0), uh[:, j * M:(j + 1) * M].bitcast(F32),
                                        ALU.subtract).then_inc(t_moved[0], 1)

            for j in range(NJ):
                name = ("ssd_out", j)
                if j >= 1:
                    to(first(name) + 3)
                    merged_low(j - 1)
                to(end(name))
                done()
                dve.wait_ge(gate_ready, NJ + j + 1)
                sg = sig_b[:, :, j * NCOL:(j + 1) * NCOL]
                Fj = F[:, :, j * NCOL:(j + 1) * NCOL]
                nc.vector.tensor_tensor(sg, tok(slot(name)), sg, ALU.mult).then_inc(evacuated[slot(name)], 1)
                dve.wait_ge(evacuated[slot(name)], moved(name))
                nc.vector.tensor_tensor(Fj, Fj, sg, ALU.add).then_inc(merged, 1)
            to(first(("mix_out", 0)) + 3)
            merged_low(NJ - 1)
            to(first(("mix_out", 0)) + 6)
            dve.wait_ge(mem_squares, T)
            inv_root(ssq_res, D)
            for t in range(T):
                nc.vector.tensor_scalar(memx[:, t], memx[:, t], sr[:, t:t + 1], None, ALU.mult).then_inc(mem_normed, 1)
            for j in range(NJ):
                to(end(("mix_out", j)))
                gained(("mix_out", j), NJ + j + 1, col=slice(j * NCOL, (j + 1) * NCOL))
                for jj, k, q in {0: ((1, 3, 0), (1, 6, 1)), 1: ((2, 1, 2), (2, 4, 3))}.get(j, ()):
                    to(first(("mix_out", jj)) + k)
                    low_area(0, ("mem", q), G_COL["mem"] + q * M, memh[:, q * M:(q + 1) * M], meml[:, q * M:(q + 1) * M])

            post_norm(2, ("mix_out", NJ - 1), pause=advance)
            pre_scale(2, advance)
            to(first("k") + 7)
            pre_low(2, 0)
            pre_low(2, 1)
            to(end("k") + 2)
            pre_low(2, 2)
            pre_low(2, 3)
            to(first("v") + 1)
            scale = float(P) ** -0.5
            for t in range(T):
                n = slice(t * X_HEADS, (t + 1) * X_HEADS)
                dve.wait_ge(t_ready[t], use(t, f"score{t}"))
                link(nc.vector.tensor_reduce(smax[:, 0, n], area(t), AX.X, ALU.max))
                nc.vector.tensor_scalar(smax[:, 1, n], smax[:, 0, n], -scale, None, ALU.mult).then_inc(max_ready, 1)
            for t in range(T):
                advance()
                advance()
                n = slice(t * X_HEADS, (t + 1) * X_HEADS)
                dve.wait_ge(probs, t + 1)
                dve.sem_inc(t_moved[t], 1)
                link(nc.vector.reciprocal(smax[:, 3, n], smax[:, 2, n]))
                nc.vector.tensor_tensor(prob[:, t], prob[:, t], smax[:, 3, n].unsqueeze(2).to_broadcast([P, X_HEADS, S]),
                                        ALU.mult).then_inc(probs_scaled, 1)
            to(end("v"))
            dve.wait_ge(o_high, 2)
            nc.vector.tensor_tensor(ol[:], feat(slot("attend")), oh[:].bitcast(F32), ALU.subtract).then_inc(evacuated[slot("attend")], 1)
            for j in range(NJ):
                to(end(("xo", j)))
                gained(("xo", j), 2 * NJ + j + 1, col=slice(j * NCOL, (j + 1) * NCOL))
            post_norm(3, ("xo", NJ - 1))
            pre_norm_behind(3)
            ffn(1)
            post_norm(4, ("down", 1, NJ - 1), 0.5)


_INS = ["x", "mem", "ffn1_pre_g", "ffn1_w1", "ffn1_w3", "ffn1_w2", "ffn1_post_g", "mix_pre_g", "w_in", "b_gate",
        "pool_w", "pool_scale", "w_pool_out", "conv_w", "conv_b", "dt_bias", "a_log", "d_skip", "ssd_norm_g",
        "w_ssd_out", "w_mix_out", "mix_post_g", "xattn_pre_g", "mem_norm_g", "w_q", "w_k", "w_v", "w_xo",
        "xattn_post_g", "ffn2_pre_g", "ffn2_w1", "ffn2_w3", "ffn2_w2", "ffn2_post_g"]


def kernel(**inputs):
    import numpy as _np
    import concourse.bacc as _bacc
    from concourse import mybir as _mybir
    from concourse.bass_utils import run_bass_kernel_spmd as _run

    seq = inputs["x"].shape[1]
    consts = {
        "identity": _np.eye(P, dtype=_np.float32),
        "causal": _np.triu(_np.ones((P, P), _np.float32)),
        "anticausal": _np.tril(_np.ones((P, P), _np.float32), -1),
        "inv_count": _np.stack([1.0 / _np.minimum(_np.arange(seq) + 1, w) for w in WINDOWS]).astype(_np.float32),
    }
    nc = _bacc.Bacc("TRN2", target_bir_lowering=False, num_devices=1)
    arrays, args = {}, []
    for name in _INS + list(consts):
        a = _np.ascontiguousarray(consts[name] if name in consts else inputs[name])
        arrays[f"in_{name}_dram"] = a
        args.append(nc.dram_tensor(f"in_{name}_dram", a.shape, _mybir.dt.from_np(a.dtype), kind="ExternalInput").ap())
    shape = inputs["x"].shape
    args.append(nc.dram_tensor("out_0_dram", shape, _mybir.dt.float32, kind="ExternalOutput").ap())
    hybrid_block(nc, *args)
    r = _run(nc, [arrays], core_ids=[0])
    return r.results[0]["out_0_dram"]
```

```python
from contextlib import ExitStack

import concourse.bass as bass
from concourse import mybir

ALU = mybir.AluOpType
ACT = mybir.ActivationFunctionType
F32 = mybir.dt.float32
F32R = mybir.dt.float32r
BF16 = mybir.dt.bfloat16
AX = mybir.AxisListType

P = 128
RING = 4
AHEAD = 3
CK = 2
NCOL = 512
EPS = 1e-6
WINDOWS = (2, 4, 8, 16)
TAPS = 4
HEAD_DIM = 64
X_HEADS = 4

KB = 1024
BASE = 16512


def hybrid_block(nc, x, mem, ffn1_pre_g, ffn1_w1, ffn1_w3, ffn1_w2, ffn1_post_g, mix_pre_g, w_in, b_gate,
                 pool_w, pool_scale, w_pool_out, conv_w, conv_b, dt_bias, a_log, d_skip, ssd_norm_g,
                 w_ssd_out, w_mix_out, mix_post_g, xattn_pre_g, mem_norm_g, w_q, w_k, w_v, w_xo,
                 xattn_post_g, ffn2_pre_g, ffn2_w1, ffn2_w3, ffn2_w2, ffn2_post_g,
                 identity, causal, anticausal, inv_count, out):
    _, S, D = x.shape
    DFF = ffn1_w1.shape[2]
    INNER = w_ssd_out.shape[1]
    CONV = conv_w.shape[2]
    HEADS = dt_bias.shape[1]
    GROUPS = (CONV - INNER) // 2 // P
    HPG = HEADS // GROUPS
    T = S // P
    KD = D // P
    M = NCOL // P
    NJ = D // NCOL
    NP = DFF // NCOL
    CD = KD // CK
    CF = DFF // P // CK
    CI = INNER // P // CK
    CX = NCOL // P // CK
    WG = HPG * HEAD_DIM
    assert T == 2 and WG == NCOL and HPG == 8 and NP % 2 == 1 and (2 * CF) % RING == 0

    jobs = {}
    names = []

    def plan(name, chunks):
        start = jobs[names[-1]][1] + jobs[names[-1]][2] if names else 0
        jobs[name] = (len(names), start, chunks)
        names.append(name)

    def plan_ffn(f):
        for j in range(NP):
            plan(("gate", f, j), CD)
            plan(("up", f, j), CD)
        for j in range(NJ):
            plan(("down", f, j), CF)

    plan_ffn(0)
    for name, n in (("pin0", CD), ("dt", 1), ("pin1", CD), ("pw0", CX), ("pin2", CD), ("pw1", CX), ("pin3", CD),
                    ("pw2", CX), ("B0", CD), ("pw3", CX)):
        plan(name, n)
    for j in range(NJ):
        plan(("gate_a", j), CD)
        plan(("pool_out", j), CD)
    for name in ("C0", "B1", "C1"):
        plan(name, CD)
    for g in range(GROUPS):
        plan(("x", g), CD)
        plan(("z", g), CD)
    for j in range(NJ):
        plan(("gate_b", j), CD)
    for j in range(NJ):
        plan(("ssd_out", j), CI)
    for j in range(NJ):
        plan(("mix_out", j), CD)
    for name in ("k", "q", "v"):
        plan(name, CD)
    plan("attend", 0)
    for j in range(NJ):
        plan(("xo", j), CX)
    plan_ffn(1)
    NCH = jobs[names[-1]][1] + jobs[names[-1]][2]

    def number(name):
        return jobs[name][0]

    def first(name):
        return jobs[name][1]

    def end(name):
        return jobs[name][1] + jobs[name][2]

    def slot(name):
        return jobs[name][0] % 2

    def moved(name):
        return jobs[name][0] // 2 + 1

    row_users = [n for n in names if isinstance(n, tuple) and n[0] in ("down", "gate_a", "gate_b", "mix_out", "xo")]

    def row_count(name):
        return 1 + [n for n in row_users if slot(n) == slot(name)].index(name)

    areas = {0: [], 1: []}
    for q in range(4):
        areas[q % 2].append(("pre0", q))
    areas[0] += [("hidden", 0, j) for j in range(NP)]
    for q in range(4):
        areas[q % 2].append(("pre1", q))
    areas[1] += ["dt", "cs", "csT", ("cb", 0), ("cb", 1), ("cb", 2), ("cb", 3)] + [("Y", g) for g in range(GROUPS)]
    for g in range(GROUPS):
        areas[0] += [("xT", g), ("yT", g)]
    areas[0] += [("merged", j) for j in range(NJ)] + [("mem", q) for q in range(4)]
    for q in range(4):
        areas[q % 2].append(("pre2", q))
    areas[0] += ["score0", "probT0"]
    areas[1] += ["score1", "probT1"]
    for q in range(4):
        areas[q % 2].append(("pre3", q))
    areas[0] += [("hidden", 1, j) for j in range(NP)]

    def use(k, name):
        return areas[k].index(name) + 1

    split_kinds = ("pre0", "pre1", "pre2", "pre3", "hidden", "merged", "mem")
    splits = {k: [n for n in areas[k] if isinstance(n, tuple) and n[0] in split_kinds] for k in (0, 1)}

    def high_use(k, name):
        return sum(1 if n[0] in ("hidden", "merged") else 2 for n in splits[k][:splits[k].index(name) + 1])

    with ExitStack() as ctx:
        def at(name, kb, shape, dt=F32):
            return nc.alloc_sbuf_tensor_at(name, shape, dt, offset=BASE + int(kb * KB))

        raw = at("raw", 0, [P, RING, CK, NCOL])
        wh = at("wh", 16, [P, RING, CK, NCOL], F32R)
        wl = at("wl", 32, [P, RING, CK, NCOL], F32R)
        res = at("res", 48, [P, T, D])
        uh = at("uh", 64, [P, KD, S], F32R)
        ul = at("ul", 80, [P, KD, S], F32R)
        hidh = at("hidh", 96, [P, DFF // P, S], F32R)
        hidl = at("hidl", 140, [P, DFF // P, S], F32R)
        silu_g = at("silu_g", 184, [P, T, NCOL])
        hid = at("hid", 188, [P, T, NCOL])
        F = at("F", 184, [P, T, D])
        mixh = at("mixh", 96, [P, KD, S], F32R)
        mixl = at("mixl", 112, [P, KD, S], F32R)
        poolh = at("poolh", 128, [P, M, S], F32R)
        pooll = at("pooll", 132, [P, M, S], F32R)
        pool_x = at("pool_x", 148, [P, M, S])
        win_a = at("win_a", 152, [P, M, S])
        win_b = at("win_b", 156, [P, M, S])
        sig_a = at("sig_a", 160, [P, T, NCOL])
        invc = at("invc", 164, [P, 4, S])
        diag = at("diag", 156, [P, T, P])
        yn = at("yn", 96, [P, INNER // P, S])
        cbm = at("cbm", 128, [P, GROUPS, 3 * P])
        bT = at("bT", 140, [P, M, S])
        cT = at("cT", 144, [P, M, S])
        E = at("E", 140, [P, HPG, 3 * P])
        csb = at("csb", 152, [P, HPG, T, P])
        xc = at("xc", 160, [P, M, S])
        X = at("X", 164, [P, T, NCOL])
        Xdt = at("Xdt", 168, [P, T, NCOL])
        zs = at("zs", 172, [P, T, NCOL])
        yb = at("yb", 176, [P, T, NCOL])
        small = at("small", 180, [P, 16, HEADS])
        DTR, AB, EX, LG, DTV, AV, CS, REM = 0, 2, 4, 6, 8, 10, 12, 14
        EA = 15
        cst = at("cst", 168, [P, P])
        upper = at("upper", 169, [P, P])
        rows = at("rows", 168, [P, 4, P])
        dtb_bc = at("dtb_bc", 172, [P, HEADS])
        alog_bc = at("alog_bc", 172.25, [P, HEADS])
        dt_rows = at("dt_rows", 172.5, [HEADS, S])
        ynh = at("ynh", 128, [P, INNER // P, S], F32R)
        ynl = at("ynl", 96, [P, INNER // P, S], F32R)
        sig_b = at("sig_b", 160, [P, T, D])
        memh = at("memh", 96, [P, KD, S], F32R)
        meml = at("meml", 112, [P, KD, S], F32R)
        memx = at("memx", 128, [P, T, D])
        mem_junk = at("mem_junk", 176, [P, D], BF16)
        kT = at("kT", 144, [P, M, S])
        V = at("V", 148, [P, T, NCOL])
        qT = at("qT", 152, [P, M, S])
        prob = at("prob", 156, [P, T, X_HEADS, S])
        probT = at("probT", 164, [P, T, X_HEADS, S])
        oh = at("oh", 172, [P, M, S], F32R)
        ol = at("ol", 176, [P, M, S], F32R)
        smax = at("smax", 180, [P, 4, T * X_HEADS])
        row_bc = at("row_bc", 200, [P, 2, NCOL])
        d_bc = at("d_bc", 204, [P, HEADS])
        ident = at("ident", 204.5, [P, P])
        tri = at("tri", 205, [P, P])
        cols = at("cols", 205.5, [P, 368])
        stat = at("stat", 206.9375, [P, 32])
        ssq_job = stat[:, 0:8].rearrange("p (t j) -> p t j", t=T)
        ssum, sv, ss, sr, ssq_res, sr_ffn = (stat[:, 8 + 2 * i:10 + 2 * i] for i in range(6))
        ssq_half = stat[:, 20:24].rearrange("p (t h) -> p t h", t=T)
        UPDATES = {1: 2 * T, 2: 2 * T, 3: NJ * T, 4: 2 * T}

        def updates_before(n):
            return sum(UPDATES[b] for b in UPDATES if b < n)

        def squares_before(n):
            return (0, T, 3 * T, 5 * T)[n]

        G_COL = {"pre0": 0, "pre1": KD, "pre2": 2 * KD, "pre3": 3 * KD, "mem": 4 * KD}
        PS_COL, NG_COL, CW_COL, CB_COL = 5 * KD, 6 * KD, 8 * KD, 8 * KD + 192

        J = ctx.enter_context(nc.psum_tensor("J", [P, 2, T, NCOL], F32))
        A = ctx.enter_context(nc.psum_tensor("A", [P, 2, T, NCOL], F32))

        def tok(s):
            return J[:, s]

        def feat(s):
            return J[:, s].rearrange("p t (a n) -> p (t a) n", n=S)

        def area(k):
            return A[:, k].rearrange("p t (a n) -> p (t a) n", n=S)

        cs_dram = nc.dram_tensor("cs_dram", [T, HEADS, P], F32).ap()

        def sem(name):
            return ctx.enter_context(nc.semaphore(name))

        loaded = [sem(f"loaded{i}") for i in range(RING)]
        high = sem("high")
        low = sem("low")
        panels = sem("panels")
        used = sem("used")
        evacuated = [sem("evacuated0"), sem("evacuated1")]
        row_loaded = [sem("row_loaded0"), sem("row_loaded1")]
        t_ready = [sem("t_ready0"), sem("t_ready1")]
        t_high = [sem("t_high0"), sem("t_high1")]
        t_moved = [sem("t_moved0"), sem("t_moved1")]
        x_loaded = [sem(f"x_loaded{q}") for q in range(4)]
        first_row_loaded = sem("first_row_loaded")
        rows_loaded = sem("rows_loaded")
        ident_loaded = sem("ident_loaded")
        consts_loaded = sem("consts_loaded")
        cols_ready = sem("cols_ready")
        job_squares = sem("job_squares")
        res_ready = sem("res_ready")
        res_squares = sem("res_squares")
        var_ready = sem("var_ready")
        root_ready = sem("root_ready")
        normed = sem("normed")
        step = sem("step")
        mix_loaded = sem("mix_loaded")
        pooled_ready = sem("pooled_ready")
        pooled_high = sem("pooled_high")
        pooled_low = sem("pooled_low")
        pw_high = sem("pw_high")
        gate_biased = sem("gate_biased")
        gate_ready = sem("gate_ready")
        dt_step = sem("dt_step")
        dt_func = sem("dt_func")
        a_ready = sem("a_ready")
        cs_stored = sem("cs_stored")
        csb_loaded = sem("csb_loaded")
        bc_silu = sem("bc_silu")
        seg_ready = sem("seg_ready")
        exp_ready = sem("exp_ready")
        w_ready = sem("w_ready")
        xc_silu = sem("xc_silu")
        xdt_ready = sem("xdt_ready")
        gated = sem("gated")
        y_squares = sem("y_squares")
        y_normed = sem("y_normed")
        yn_high = sem("yn_high")
        yn_low = sem("yn_low")
        merged = sem("merged")
        mem_loaded = sem("mem_loaded")
        mem_squares = sem("mem_squares")
        mem_normed = sem("mem_normed")
        max_ready = sem("max_ready")
        probs = sem("probs")
        probs_scaled = sem("probs_scaled")
        v_moved = sem("v_moved")
        attended = sem("attended")
        o_high = sem("o_high")
        o_low = sem("o_low")
        stored = sem("stored")

        def lin(static, i, per):
            return static if i is None else i * per + static

        def panel(w, k, col):
            return w[k * CK * P:(k + 1) * CK * P, col].rearrange("(k p) n -> p k n", p=P)

        C1 = D + INNER
        C3 = C1 + CONV + HEADS
        W_IN = w_in[0]

        block = ctx.enter_context(nc.Block())

        @block.sync
        def _(sp):
            sp.dma_start(ident[:], identity).then_inc(ident_loaded, 16)

            chunk = [0]

            def load(src, i=None, per=0, view=None, top=False):
                c = chunk[0]
                r = c % RING
                if i is not None or c >= RING:
                    sp.wait_ge(low, lin(c - RING + 1, i, per))
                if top and i is not None:
                    sp.sem_inc(panels, 1)
                dst = raw[:, r] if view is None else view(r)
                sp.dma_start(dst, src).then_inc(loaded[r], 16)
                chunk[0] += 1

            def load_job(w, col, n, i=None, per=0, ahead=lambda k: None):
                for k in range(n):
                    ahead(k)
                    load(panel(w, k, col), i, per, top=(k == 0))

            def load_x(k):
                if k < 4:
                    c = slice(k * NCOL, (k + 1) * NCOL)
                    sp.dma_start(res[:, :, c], x[0].rearrange("(t p) d -> p t d", p=P)[:, :, c]).then_inc(x_loaded[k], 16)

            def ffn(f, w1, w3, w2, first_ahead=lambda k: None):
                load_job(w1[0], slice(0, NCOL), CD, ahead=first_ahead)
                if f == 0:
                    sp.dma_start(tri[:], causal).then_inc(consts_loaded, 16)
                    sp.dma_start(d_bc[:], d_skip[0:1, :].to_broadcast([P, HEADS])).then_inc(consts_loaded, 16)
                load_job(w3[0], slice(0, NCOL), CD)
                with sp.Fori(1, NP) as j:
                    chunk[0] = first(("gate", f, 0))
                    load_job(w1[0], bass.ds(j * NCOL, NCOL), CD, j, 2 * CD)
                    load_job(w3[0], bass.ds(j * NCOL, NCOL), CD, j, 2 * CD)
                chunk[0] = first(("down", f, 0))
                with sp.Fori(0, NJ // 2) as i:
                    for o in range(2):
                        col = bass.ds(i * (2 * NCOL) + o * NCOL, NCOL)
                        load_job(w2[0], col, CF, i, 2 * CF)
                chunk[0] = end(("down", f, NJ - 1))

            ffn(0, ffn1_w1, ffn1_w3, ffn1_w2, load_x)

            def cols_at(c):
                return slice(c, c + NCOL)

            for name in ("pin0", "dt", "pin1", "pw0", "pin2", "pw1", "pin3", "pw2", "B0", "pw3"):
                if name == "B0":
                    load_job(W_IN, cols_at(C1 + INNER), CD)
                elif name == "dt":
                    load(W_IN[:, C1 + CONV:C3].rearrange("(k p) n -> p k n", p=P),
                         view=lambda r: raw[:, r].rearrange("p k n -> p (k n)").rearrange("p (k n) -> p k n", n=HEADS))
                else:
                    g = int(name[-1])
                    if name[:3] == "pin":
                        load_job(W_IN, cols_at(g * NCOL), CD)
                    else:
                        load_job(pool_w[0, g], cols_at(0), CX)
            with sp.Fori(0, NJ) as j:
                chunk[0] = first(("gate_a", 0))
                load_job(W_IN, bass.ds(j * NCOL + C3, NCOL), CD, j, 2 * CD)
                load_job(w_pool_out[0], bass.ds(j * NCOL, NCOL), CD, j, 2 * CD)
            chunk[0] = first("C0")
            load_job(W_IN, cols_at(C1 + INNER + GROUPS * P), CD)
            load_job(W_IN, cols_at(C1 + INNER + NCOL), CD)
            load_job(W_IN, cols_at(C1 + INNER + GROUPS * P + NCOL), CD)
            with sp.Fori(0, GROUPS) as g:
                chunk[0] = first(("x", 0))
                load_job(W_IN, bass.ds(g * NCOL + C1, NCOL), CD, g, 2 * CD)
                load_job(W_IN, bass.ds(g * NCOL + D, NCOL), CD, g, 2 * CD)
            chunk[0] = first(("gate_b", 0))
            for j in range(NJ):
                load_job(W_IN, cols_at(C3 + D + j * NCOL), CD)
            with sp.Fori(0, NJ) as j:
                chunk[0] = first(("ssd_out", 0))
                load_job(w_ssd_out[0], bass.ds(j * NCOL, NCOL), CI, j, CI)
            chunk[0] = first(("mix_out", 0))
            for j in range(NJ):
                load_job(w_mix_out[0], cols_at(j * NCOL), CD)
            for w in (w_k, w_q, w_v):
                load_job(w[0], cols_at(0), CD)
            for j in range(NJ):
                load_job(w_xo[0], cols_at(j * NCOL), CX)
            ffn(1, ffn2_w1, ffn2_w3, ffn2_w2)
            assert chunk[0] == NCH
            for n in range(2 * T):
                t, c = n // 2, slice(n % 2 * D // 2, (n % 2 + 1) * D // 2)
                sp.wait_ge(res_ready, updates_before(4) + n + 1)
                sp.dma_start(out[0, t * P:(t + 1) * P, c], res[:, t, c]).then_inc(stored, 16)
            sp.wait_ge(stored, 16 * 2 * T)

        @block.gpsimd
        def _(pool):
            def load_row(name, src, i=None):
                s = slot(name)
                pool.wait_ge(evacuated[s], lin(number(name) // 2, i, 1))
                pool.dma_start(row_bc[:, s], src.to_broadcast([P, NCOL])).then_inc(row_loaded[s], 16)

            def down_rows(f, g):
                with pool.Fori(0, NJ // 2) as i:
                    for o in range(2):
                        load_row(("down", f, o), g[0:1, bass.ds(i * (2 * NCOL) + o * NCOL, NCOL)], i)

            for n, g in enumerate((mix_pre_g, xattn_pre_g, ffn2_pre_g, mem_norm_g, pool_scale)):
                pool.dma_start(rows[(n + 1) * KD:(n + 2) * KD, 0, :], g[0].rearrange("(b p) -> b p", p=P)).then_inc(rows_loaded, 16)
            pool.dma_start(rows[6 * KD:8 * KD, 0, :], ssd_norm_g[0].rearrange("(b p) -> b p", p=P)).then_inc(rows_loaded, 16)
            cw = conv_w[0].rearrange("a (b p) -> (a b) p", p=P)
            nb = CONV // P
            for n in range(2):
                pool.dma_start(rows[0:2 * nb, 1 + n, :], cw[2 * nb * n:2 * nb * (n + 1), :]).then_inc(rows_loaded, 16)
            pool.dma_start(rows[0:nb, 3, :], conv_b[0].rearrange("(b p) -> b p", p=P)).then_inc(rows_loaded, 16)
            down_rows(0, ffn1_post_g)
            pool.wait_ge(used, end(("down", 0, NJ - 1)))
            pool.dma_start(dtb_bc[:], dt_bias[0:1, :].to_broadcast([P, HEADS])).then_inc(mix_loaded, 16)
            pool.dma_start(alog_bc[:], a_log[0:1, :].to_broadcast([P, HEADS])).then_inc(mix_loaded, 16)
            pool.dma_start(upper[:], anticausal).then_inc(mix_loaded, 16)
            pool.dma_start(invc[:], inv_count.rearrange("(o w) n -> o w n", o=1).to_broadcast([P, 4, S])).then_inc(mix_loaded, 16)
            pool.wait_ge(t_moved[1], use(1, "csT"))
            pool.dma_start(cs_dram.rearrange("t h n -> (t h) n"), cst[:]).then_inc(cs_stored, 16)
            pool.wait_ge(cs_stored, 16)
            pool.wait_ge(pooled_low, len(WINDOWS))

            def load_csb(g):
                for t in range(T):
                    pool.dma_start(csb[:, :, t, :], cs_dram[t:t + 1, bass.ds(g * HPG, HPG), :].to_broadcast([P, HPG, P])).then_inc(csb_loaded, 16)

            load_csb(0)
            with pool.Fori(0, NJ) as j:
                load_row(("gate_a", 0), b_gate[0:1, bass.ds(j * NCOL, NCOL)], j)
            with pool.Fori(1, GROUPS) as g:
                pool.wait_ge(seg_ready, g)
                load_csb(g)
            for j in range(NJ):
                load_row(("gate_b", j), b_gate[0:1, D + j * NCOL:D + (j + 1) * NCOL])
            pool.wait_ge(used, end(("ssd_out", NJ - 1)))
            pool.dma_start(memx[:], mem[0].rearrange("(t p) d -> p t d", p=P)).then_inc(mem_loaded, 16)
            for j in range(NJ):
                load_row(("mix_out", j), mix_post_g[0:1, j * NCOL:(j + 1) * NCOL])
            for j in range(NJ):
                load_row(("xo", j), xattn_post_g[0:1, j * NCOL:(j + 1) * NCOL])
            down_rows(1, ffn2_post_g)

        @block.tensor
        def _(pe):
            chunk = [0]

            def take(i=None, per=0):
                c = chunk[0]
                pe.wait_ge(high, lin(c + 1, i, per))
                pe.wait_ge(low, lin(c + 1, i, per))
                chunk[0] += 1
                return c % RING

            def claim(name, i=None, per=1):
                n = number(name)
                if n >= 2:
                    pe.wait_ge(evacuated[n % 2], lin(n // 2, i, per))

            def token_chunks(name, xh, xl, ks, last_k, i=None, per=0, before=None):
                o = tok(slot(name))
                for k in ks:
                    if before is not None:
                        before(k)
                    r = take(i, per)
                    for kk in range(CK):
                        for t in range(T):
                            a, b = xh[:, k * CK + kk, t * P:(t + 1) * P], xl[:, k * CK + kk, t * P:(t + 1) * P]
                            nc.tensor.matmul(o[:, t], b, wh[:, r, kk], start=(k == 0 and kk == 0), stop=False)
                            nc.tensor.matmul(o[:, t], a, wh[:, r, kk], start=False, stop=False)
                            mm = nc.tensor.matmul(o[:, t], a, wl[:, r, kk], start=False,
                                                  stop=(k == last_k and kk == CK - 1))
                    mm.then_inc(used, 1)

            def feature_chunks(name, xh, xl, ks, last_k, i=None, per=0, before=None):
                o = feat(slot(name))
                for k in ks:
                    if before is not None:
                        before(k)
                    r = take(i, per)
                    for kk in range(CK):
                        a, b = xh[:, k * CK + kk], xl[:, k * CK + kk]
                        for m in range(M):
                            h, l = wh[:, r, kk, m * P:(m + 1) * P], wl[:, r, kk, m * P:(m + 1) * P]
                            nc.tensor.matmul(o[:, m], h, b, start=(k == 0 and kk == 0 and m % 2 == 0), stop=False,
                                             skip_group_check=True)
                            nc.tensor.matmul(o[:, m], h, a, start=False, stop=False, skip_group_check=True)
                            mm = nc.tensor.matmul(o[:, m], l, a, start=False,
                                                  stop=(k == last_k and kk == CK - 1), skip_group_check=True)
                    mm.then_inc(used, 1)

            def claim_area(k, name, i=None, per=1):
                n = use(k, name) - 1
                if n >= 1:
                    pe.wait_ge(t_moved[k], lin(n, i, per))

            def turn(k, src):
                o = area(k)
                for m in range(M):
                    for t in range(T):
                        tr = nc.tensor.transpose(o[:, m, t * P:(t + 1) * P], src[:, t, m * P:(m + 1) * P], ident[:])
                tr.then_inc(t_ready[k], 1)

            def turn_pre(n, qs):
                for q in qs:
                    claim_area(q % 2, (f"pre{n}", q))
                    for t in range(T):
                        pe.wait_ge(normed, 1 + T * (n - 1) + t + 1)
                        for m in range(M):
                            c = slice(q * NCOL + m * P, q * NCOL + (m + 1) * P)
                            mm = nc.tensor.matmul(area(q % 2)[:, m, t * P:(t + 1) * P], res[:, t, c], diag[:, t],
                                                  start=True, stop=True, skip_group_check=True)
                        if t == T - 1:
                            mm.then_inc(t_ready[q % 2], 1)

            def turn_res(n, qs):
                for q in qs:
                    if n == 0:
                        pe.wait_ge(x_loaded[q], 16)
                    else:
                        pe.wait_ge(res_ready, updates_before(n) + T * (q + 1))
                    claim_area(q % 2, (f"pre{n}", q))
                    turn(q % 2, res[:, :, q * NCOL:(q + 1) * NCOL])

            def pre_wait(n):
                def before(k):
                    if k % 2 == 0:
                        q = k // 2
                        pe.wait_ge(t_moved[q % 2], use(q % 2, (f"pre{n}", q)))
                return before

            def turn_rows():
                pe.wait_ge(rows_loaded, 16 * 9)
                widths = (P, 96, 96, 48)
                for n, wd in enumerate(widths):
                    tr = nc.tensor.transpose(J[:, 1, 0, sum(widths[:n]):sum(widths[:n + 1])], rows[0:wd, n, :], ident[0:wd, 0:wd])
                tr.then_inc(cols_ready, 1)

            def ffn(f):
                def turn_hidden(j, i=None):
                    pe.wait_ge(evacuated[slot(("up", f, 0))], lin(moved(("up", f, j)), i, 1))
                    claim_area(0, ("hidden", f, j), i)
                    turn(0, hid)

                def pair(i=None):
                    chunk[0] = first(("gate", f, 0))
                    claim(("gate", f, 0), i)
                    n = {0: 0, 1: 3}[f]
                    if i is None and f == 1:
                        turn_res(n, (0, 1))
                    before = pre_wait(n) if i is None else None
                    token_chunks(("gate", f, 0), uh, ul, range(0, 2), CD - 1, i, 2 * CD, before)
                    if i is None:
                        turn_res(n, (2, 3))
                        if f == 0:
                            turn_rows()
                    token_chunks(("gate", f, 0), uh, ul, range(2, 3), CD - 1, i, 2 * CD, before)
                    if i is not None:
                        turn_hidden(0, i - 1)
                    token_chunks(("gate", f, 0), uh, ul, range(3, CD), CD - 1, i, 2 * CD, before)
                    if i is None and f == 0:
                        pe.wait_ge(cols_ready, 4)
                    claim(("up", f, 0), i)
                    token_chunks(("up", f, 0), uh, ul, range(CD), CD - 1, i, 2 * CD)

                pair()
                with pe.Fori(1, NP) as j:
                    pair(j)
                turn_hidden(NP - 1)
                with pe.Fori(0, NJ // 2) as i:
                    chunk[0] = first(("down", f, 0))
                    for o in range(2):
                        claim(("down", f, o), i)
                        token_chunks(("down", f, o), hidh, hidl, range(CF - 2), CF - 1, i, 2 * CF)
                        pe.wait_ge(t_moved[0], use(0, ("hidden", f, NP - 1)))
                        token_chunks(("down", f, o), hidh, hidl, range(CF - 2, CF), CF - 1, i, 2 * CF)
                chunk[0] = end(("down", f, NJ - 1))

            pe.wait_ge(ident_loaded, 16)
            turn_res(0, (0,))
            pe.wait_ge(first_row_loaded, 16)
            nc.tensor.transpose(J[:, 0, 0, 0:KD], rows[0:KD, 0, :], ident[0:KD, 0:KD]).then_inc(cols_ready, 1)
            turn_res(0, (1,))
            pe.wait_ge(cols_ready, 2)
            ffn(0)

            claim("pin0")
            turn_pre(1, (0, 1))
            feature_chunks("pin0", uh, ul, range(0, 2), CD - 1, before=pre_wait(1))
            turn_pre(1, (2, 3))
            feature_chunks("pin0", uh, ul, range(2, CD), CD - 1, before=pre_wait(1))
            claim("dt")
            r = take()
            o = J[0:HEADS, slot("dt"), 0, 0:S]
            wdh = wh[:, r].rearrange("p k n -> p (k n)").rearrange("p (k n) -> p k n", n=HEADS)
            wdl = wl[:, r].rearrange("p k n -> p (k n)").rearrange("p (k n) -> p k n", n=HEADS)
            for k in range(KD):
                nc.tensor.matmul(o, wdh[:, k], ul[:, k], start=(k == 0), stop=False)
                nc.tensor.matmul(o, wdh[:, k], uh[:, k], start=False, stop=False)
                mm = nc.tensor.matmul(o, wdl[:, k], uh[:, k], start=False, stop=(k == KD - 1))
            mm.then_inc(used, 1)

            def feature_job(name, xh=uh, xl=ul, n=CD):
                claim(name)
                feature_chunks(name, xh, xl, range(n), n - 1)

            claim("pin1")
            feature_chunks("pin1", uh, ul, range(0, 1), CD - 1)
            pe.wait_ge(evacuated[slot("dt")], moved("dt"))
            claim_area(1, "dt")
            for t in range(T):
                tr = nc.tensor.transpose(A[:, 1, 0, t * HEADS:(t + 1) * HEADS], dt_rows[:, t * P:(t + 1) * P], ident[0:HEADS, 0:HEADS])
            tr.then_inc(t_ready[1], 1)
            feature_chunks("pin1", uh, ul, range(1, 7), CD - 1)
            pe.wait_ge(a_ready, 1)
            pe.wait_ge(mix_loaded, 64)
            pe.wait_ge(consts_loaded, 32)
            claim_area(1, "cs")
            nc.tensor.matmul(A[:, 1, 0, 0:T * HEADS], tri[:], small[:, AV:AV + T], start=True, stop=True)
            nc.tensor.matmul(A[:, 1, 1, 0:HEADS], upper[:], small[:, AV], start=True, stop=True).then_inc(t_ready[1], 1)
            feature_chunks("pin1", uh, ul, range(7, CD), CD - 1)
            claim_area(1, "csT")
            nc.tensor.transpose(A[:, 1, 0, 0:P], small[:, CS:CS + T].rearrange("p t h -> p (t h)"), ident[:]).then_inc(t_ready[1], 1)
            for name in ("pw0", "pin2", "pw1", "pin3", "pw2", "B0", "pw3"):
                if name[:2] == "pw":
                    pe.wait_ge(pooled_low, int(name[-1]) + 1)
                    feature_job(name, poolh, pooll, CX)
                else:
                    feature_job(name)
            with pe.Fori(0, NJ) as j:
                chunk[0] = first(("gate_a", 0))
                claim(("gate_a", 0), j)
                token_chunks(("gate_a", 0), uh, ul, range(CD), CD - 1, j, 2 * CD)
                claim(("pool_out", 0), j)
                token_chunks(("pool_out", 0), mixh, mixl, range(CD), CD - 1, j, 2 * CD)
            chunk[0] = first("C0")
            feature_job("C0")

            def cb(half, pair):
                pe.wait_ge(bc_silu, 2 * half + 2)
                claim_area(1, ("cb", 2 * half + pair))
                for q in range(2):
                    m = 2 * pair + q
                    nc.tensor.matmul(A[:, 1, q, 0:S], bT[:, m, 0:P], cT[:, m, :], start=True, stop=True)
                    mm = nc.tensor.matmul(A[:, 1, q, S:S + P], bT[:, m, P:S], cT[:, m, P:S], start=True, stop=True)
                mm.then_inc(t_ready[1], 1)

            claim("B1")
            feature_chunks("B1", uh, ul, range(0, 5), CD - 1)
            cb(0, 0)
            feature_chunks("B1", uh, ul, range(5, 6), CD - 1)
            cb(0, 1)
            feature_chunks("B1", uh, ul, range(6, CD), CD - 1)
            feature_job("C1")

            def turn_y(g0, i=None):
                pe.wait_ge(y_normed, lin(g0 + 1, i, 1))
                claim_area(0, ("yT", g0), i, 2)
                turn(0, yb)

            def group(i=None):
                chunk[0] = first(("x", 0))
                per = 2 * CD
                claim(("x", 0), i)
                feature_chunks(("x", 0), uh, ul, range(0, 6), CD - 1, i, per)
                if i is None:
                    cb(1, 0)
                else:
                    turn_y(0, i - 1)
                feature_chunks(("x", 0), uh, ul, range(6, 7), CD - 1, i, per)
                if i is None:
                    cb(1, 1)
                feature_chunks(("x", 0), uh, ul, range(7, CD), CD - 1, i, per)
                claim(("z", 0), i)
                token_chunks(("z", 0), uh, ul, range(0, 5), CD - 1, i, per)
                pe.wait_ge(xc_silu, lin(1, i, 1))
                claim_area(0, ("xT", 0), i, 2)
                for t in range(T):
                    for m in range(M):
                        tr = nc.tensor.transpose(A[:, 0, t, m * P:(m + 1) * P], xc[:, m, t * P:(t + 1) * P], ident[:])
                tr.then_inc(t_ready[0], 1)
                token_chunks(("z", 0), uh, ul, range(5, CD), CD - 1, i, per)
                pe.wait_ge(w_ready, lin(1, i, 1))
                pe.wait_ge(xdt_ready, lin(1, i, 1))
                claim_area(1, ("Y", 0), i)
                for h in range(HPG):
                    c = slice(h * HEAD_DIM, (h + 1) * HEAD_DIM)
                    nc.tensor.matmul(A[:, 1, 0, c], E[:, h, 0:P], Xdt[:, 0, c], start=True, stop=True)
                    nc.tensor.matmul(A[:, 1, 1, c], E[:, h, P:2 * P], Xdt[:, 0, c], start=True, stop=False)
                    mm = nc.tensor.matmul(A[:, 1, 1, c], E[:, h, 2 * P:3 * P], Xdt[:, 1, c], start=False, stop=True)
                mm.then_inc(t_ready[1], 1)

            group()
            with pe.Fori(1, GROUPS) as g:
                group(g)
            chunk[0] = first(("gate_b", 0))
            for j in range(NJ):
                claim(("gate_b", j))
                token_chunks(("gate_b", j), uh, ul, range(0, 6), CD - 1)
                if j == 0:
                    turn_y(GROUPS - 1)
                token_chunks(("gate_b", j), uh, ul, range(6, CD), CD - 1)
            pe.wait_ge(yn_low, GROUPS)

            def turn_merged(j):
                pe.wait_ge(merged, NJ + j + 1)
                claim_area(0, ("merged", j))
                turn(0, F[:, :, j * NCOL:(j + 1) * NCOL])

            for j in range(NJ):
                claim(("ssd_out", j))
                token_chunks(("ssd_out", j), ynh, ynl, range(0, 3), CI - 1)
                if j >= 1:
                    turn_merged(j - 1)
                token_chunks(("ssd_out", j), ynh, ynl, range(3, CI), CI - 1)
            for j in range(NJ):
                claim(("mix_out", j))
                if j == 0:
                    pe.wait_ge(t_moved[0], use(0, ("merged", NJ - 2)))
                for k in range(CD):
                    if j == 0 and k == 3:
                        turn_merged(NJ - 1)
                    if j == 0 and k == CD - 2:
                        pe.wait_ge(t_moved[0], use(0, ("merged", NJ - 1)))
                    if (j, k) in ((1, 3), (1, 6), (2, 1), (2, 4)):
                        q = ((1, 3), (1, 6), (2, 1), (2, 4)).index((j, k))
                        pe.wait_ge(mem_normed, T)
                        claim_area(0, ("mem", q))
                        turn(0, memx[:, :, q * NCOL:(q + 1) * NCOL])
                    token_chunks(("mix_out", j), uh, ul, range(k, k + 1), CD - 1)

            pe.wait_ge(t_moved[0], use(0, ("mem", 3)))
            claim("k")
            feature_chunks("k", memh, meml, range(0, 7), CD - 1)
            turn_pre(2, (0, 1))
            feature_chunks("k", memh, meml, range(7, CD), CD - 1)
            claim("q")
            feature_chunks("q", uh, ul, range(0, 2), CD - 1, before=pre_wait(2))
            turn_pre(2, (2, 3))
            feature_chunks("q", uh, ul, range(2, CD), CD - 1, before=pre_wait(2))
            claim("v")
            token_chunks("v", memh, meml, range(0, 1), CD - 1)
            pe.wait_ge(evacuated[slot("k")], moved("k"))
            pe.wait_ge(evacuated[slot("q")], moved("q"))
            for t in range(T):
                claim_area(t, f"score{t}")
                for h in range(X_HEADS):
                    mm = nc.tensor.matmul(area(t)[:, h], qT[:, h, t * P:(t + 1) * P], kT[:, h], start=True, stop=True)
                mm.then_inc(t_ready[t], 1)
            token_chunks("v", memh, meml, range(1, 7), CD - 1)
            pe.wait_ge(probs_scaled, T)
            for mt in range(T):
                claim_area(mt, f"probT{mt}")
                for h in range(X_HEADS):
                    for t in range(T):
                        tr = nc.tensor.transpose(area(mt)[:, h, t * P:(t + 1) * P], prob[:, t, h, mt * P:(mt + 1) * P], ident[:])
                tr.then_inc(t_ready[mt], 1)
            token_chunks("v", memh, meml, range(7, CD), CD - 1)
            claim("attend")
            pe.wait_ge(v_moved, 1)
            for mt in range(T):
                pe.wait_ge(t_moved[mt], use(mt, f"probT{mt}"))
            for h in range(X_HEADS):
                if h == X_HEADS // 2:
                    pe.wait_ge(evacuated[slot("v")], moved("v"))
                for mt in range(T):
                    mm = nc.tensor.matmul(feat(slot("attend"))[:, h], V[:, mt, h * P:(h + 1) * P], probT[:, mt, h],
                                          start=(mt == 0), stop=(mt == T - 1), skip_group_check=True)
                if h % 2 == 1:
                    mm.then_inc(attended, 1)
            pe.wait_ge(o_low, 1)
            for j in range(NJ):
                claim(("xo", j))
                token_chunks(("xo", j), oh, ol, range(0, 1), CX - 1)
                if j == 0:
                    pe.wait_ge(evacuated[slot("attend")], moved("attend"))
                token_chunks(("xo", j), oh, ol, range(1, CX), CX - 1)

            ffn(1)
            assert chunk[0] == NCH

        @block.scalar
        def _(act):
            at_chunk = [0]
            act.dma_start(rows[0:KD, 0, :], ffn1_pre_g[0].rearrange("(b p) -> b p", p=P)).then_inc(first_row_loaded, 16)

            def advance(i=None, per=0):
                c = at_chunk[0] + AHEAD
                at_chunk[0] += 1
                if c < NCH:
                    r = c % RING
                    act.wait_ge(loaded[r], lin(16 * (c // RING + 1), i, 16 * per // RING))
                    if i is not None or c >= RING:
                        act.wait_ge(used, lin(c - RING + 1, i, per))
                    nc.scalar.activation(wh[:, r], raw[:, r], ACT.Copy).then_inc(high, 1)

            def to(n, i=None, per=0):
                assert at_chunk[0] <= n, (at_chunk[0], n)
                while at_chunk[0] < n:
                    advance(i, per)

            def done(i=None, per=0):
                act.wait_ge(used, lin(at_chunk[0], i, per))

            def first_split(r):
                act.wait_ge(loaded[r], 16)
                nc.scalar.activation(wh[:, r], raw[:, r], ACT.Copy).then_inc(high, 1)

            roots = [0]

            def root(n, i=None, ap=slice(0, T)):
                act.wait_ge(var_ready, lin(n, i, 1))
                nc.scalar.activation(ss[:, ap], sv[:, ap], ACT.Sqrt).then_inc(root_ready, 1)

            def fetch_root(n):
                nc.scalar.activation(stat[:, 28 + n:29 + n], ident[:, 0:1], ACT.Sqrt)

            def next_root(ap=slice(0, T)):
                roots[0] += 1
                root(roots[0], None, ap)

            def job_square(name, n, col):
                act.wait_ge(job_squares, n)
                for t in range(T):
                    sq = nc.scalar.activation(A[:, 1, t], tok(slot(name))[:, t], ACT.Square, accum_out=ssq_job[:, t, col])
                sq.then_inc(job_squares, 1)

            def split_area(k, name, gain, dst):
                act.wait_ge(t_ready[k], use(k, name))
                for m in range(M):
                    a = nc.scalar.activation(dst[:, m], area(k)[:, m], ACT.Copy, scale=cols[:, gain + m:gain + m + 1])
                    if m % 2 == 1:
                        a.then_inc(t_high[k], 1)

            def pre_high(n, q):
                split_area(q % 2, (f"pre{n}", q), G_COL[f"pre{n}"] + q * M, uh[:, q * M:(q + 1) * M])

            def res_square(n, t):
                if n == 0:
                    for q in range(4):
                        act.wait_ge(x_loaded[q], 16)
                else:
                    act.wait_ge(res_ready, updates_before(n + 1))
                nc.scalar.activation(F[:, t], res[:, t], ACT.Square, accum_out=ssq_res[:, t:t + 1]).then_inc(res_squares, 1)

            def half_square(n, t, h):
                act.wait_ge(res_ready, updates_before(n) + 2 * t + h + 1)
                c = slice(h * D // 2, (h + 1) * D // 2)
                nc.scalar.activation(F[:, t, c], res[:, t, c], ACT.Square, accum_out=ssq_half[:, t, h:h + 1]).then_inc(res_squares, 1)

            def pre_norm(n):
                for t in range(T):
                    for h in range(2):
                        half_square(n, t, h)
                    next_root(slice(t, t + 1))
                for q in range(4):
                    pre_high(n, q)

            def pre_norm_behind(n, first_splits=lambda r: None):
                first_splits(0)
                pre_high(n, 0)
                first_splits(1)
                pre_high(n, 1)
                first_splits(2)
                advance()
                pre_high(n, 2)
                advance()
                pre_high(n, 3)
                advance()
                for t in range(T):
                    res_square(n, t)
                next_root()

            def ffn(f):
                def silu(i=None):
                    done(i, 2 * CD)
                    if i is not None:
                        act.wait_ge(evacuated[slot(("up", f, 0))], lin(moved(("up", f, 0)), i - 1, 1))
                    if i is None:
                        act.wait_ge(normed, {0: 1, 1: 2 * T + 2}[f])
                    for t in range(T):
                        a = nc.scalar.activation(silu_g[:, t], tok(slot(("gate", f, 0)))[:, t], ACT.Silu, scale=sr_ffn[:, t:t + 1])
                    a.then_inc(evacuated[slot(("gate", f, 0))], 1)

                def hidden_high(i=None, j=0):
                    act.wait_ge(t_ready[0], lin(use(0, ("hidden", f, j)), i, 1))
                    dst = hidh[:, j * M:(j + 1) * M] if i is None else hidh[:, bass.ds(i * M, M)]
                    nc.scalar.activation(dst, area(0), ACT.Copy).then_inc(t_high[0], 1)

                c0 = first(("gate", f, 0))

                def pair(i=None):
                    if i is not None:
                        at_chunk[0] = c0
                    to(c0 + 3, i, 2 * CD)
                    if i is not None:
                        hidden_high(i - 1)
                    to(c0 + CD, i, 2 * CD)
                    silu(i)
                    to(c0 + 2 * CD, i, 2 * CD)

                pair()
                with act.Fori(1, NP) as j:
                    pair(j)
                at_chunk[0] = first(("down", f, 0))
                hidden_high(None, NP - 1)
                fetch_root(1 + f)
                d0 = first(("down", f, 0))

                if f == 0:
                    with act.Fori(0, NJ // 2) as i:
                        at_chunk[0] = d0
                        for o in range(2):
                            to(d0 + (o + 1) * CF, i, 2 * CF)
                            done(i, 2 * CF)
                            before = names[number(("down", f, o)) - 1]
                            act.wait_ge(evacuated[slot(before)], i + moved(before))
                            for t in range(T):
                                sq = nc.scalar.activation(A[:, 1, t], tok(slot(("down", f, o)))[:, t], ACT.Square,
                                                          accum_out=ssq_job[:, t, bass.ds(i * 2 + o, 1)])
                            sq.then_inc(job_squares, 1)
                    at_chunk[0] = end(("down", f, NJ - 1))
                else:
                    for j in range(NJ):
                        to(end(("down", f, j)))
                        done()
                        job_square(("down", f, j), 3 * NJ + j, slice(j, j + 1))

            act.wait_ge(ident_loaded, 16)
            fetch_root(0)
            act.wait_ge(cols_ready, 2)
            pre_norm_behind(0, first_split)
            ffn(0)
            next_root()
            pre_norm(1)
            to(end("pin0"))
            done()
            nc.scalar.activation(pool_x[:], feat(slot("pin0")), ACT.Copy).then_inc(evacuated[slot("pin0")], 1)

            to(end("dt") + 2)
            act.wait_ge(mix_loaded, 64)
            nc.scalar.activation(small[:, EA], alog_bc[:], ACT.Exp).then_inc(dt_func, 1)
            act.wait_ge(t_moved[1], use(1, "dt"))
            nc.scalar.activation(small[:, EX:EX + T], small[:, DTR:DTR + T], ACT.Abs).then_inc(dt_func, 1)
            act.wait_ge(dt_func, 2)
            nc.scalar.activation(small[:, EX:EX + T], small[:, EX:EX + T], ACT.Exp, scale=-1.0).then_inc(dt_func, 1)
            to(end("dt") + 3)
            act.wait_ge(dt_step, 1)
            nc.scalar.activation(small[:, LG:LG + T], small[:, AB:AB + T], ACT.Ln).then_inc(dt_func, 1)

            def pool_in(g):
                to(end(f"pin{g}"))
                done()
                act.wait_ge(pooled_ready, g)
                nc.scalar.activation(pool_x[:], feat(slot(f"pin{g}")), ACT.Copy).then_inc(evacuated[slot(f"pin{g}")], 1)

            def pool_high(g):
                act.wait_ge(pooled_ready, g + 1)
                if g >= 1:
                    act.wait_ge(used, end(f"pw{g - 1}"))
                nc.scalar.activation(poolh[:], win_a[:], ACT.Copy).then_inc(pooled_high, 1)

            def pool_mixed(g):
                to(end(f"pw{g}"))
                done()
                for m in range(M):
                    c = PS_COL + g * M + m
                    a = nc.scalar.activation(mixh[:, g * M + m], feat(slot(f"pw{g}"))[:, m], ACT.Copy, scale=cols[:, c:c + 1])
                a.then_inc(pw_high, 1)

            to(end("dt") + 3)
            pool_high(0)
            pool_in(1)
            pool_mixed(0)
            to(end("pw0") + 3)
            pool_high(1)
            pool_in(2)
            pool_mixed(1)
            to(end("pw1") + 3)
            pool_high(2)
            pool_in(3)
            pool_mixed(2)
            to(end("pw2") + 3)
            pool_high(3)

            def conv_silu(name, dst, n, i=None, per=0):
                act.wait_ge(evacuated[slot(name)], lin(moved(name), i, 1))
                nc.scalar.activation(dst, dst, ACT.Silu).then_inc(n, 1)

            pool_mixed(3)
            c0 = first(("gate_a", 0))
            with act.Fori(0, NJ) as j:
                at_chunk[0] = c0
                to(c0 + CD + 1, j, 2 * CD)
                act.wait_ge(gate_biased, j + 1)
                nc.scalar.activation(sig_a[:], sig_a[:], ACT.Sigmoid).then_inc(gate_ready, 1)
                to(c0 + 2 * CD, j, 2 * CD)
            at_chunk[0] = first("C0")
            conv_silu("B0", bT[:], bc_silu)
            to(end("C0") + 4)
            conv_silu("C0", cT[:], bc_silu)
            to(end("B1") + 4)
            conv_silu("B1", bT[:], bc_silu)
            to(end("C1"))

            def finish_square(g0, i=None):
                act.wait_ge(gated, lin(g0 + 1, i, 1))
                for t in range(T):
                    sq = nc.scalar.activation(zs[:, t], yb[:, t], ACT.Square, accum_out=ssq_res[:, t:t + 1])
                sq.then_inc(y_squares, 1)

            def finish_z(g0, i=None):
                act.wait_ge(used, lin(end(("z", g0)), i, 2 * CD))
                if i is not None or g0 >= 1:
                    act.wait_ge(root_ready, lin(g_root + g0, i, 1))
                nc.scalar.activation(zs[:], tok(slot(("z", 0))), ACT.Silu).then_inc(evacuated[slot(("z", 0))], 1)

            def finish_y(g0, i=None):
                act.wait_ge(t_ready[0], lin(use(0, ("yT", g0)), i, 2))
                for m in range(M):
                    if i is None:
                        dst, sc = yn[:, g0 * M + m], cols[:, NG_COL + g0 * M + m:NG_COL + g0 * M + m + 1]
                    else:
                        dst = yn[:, bass.ds(i * M + (g0 * M + m), 1)].rearrange("p a n -> p (a n)")
                        sc = cols[:, bass.ds(i * M + (NG_COL + g0 * M + m), 1)]
                    a = nc.scalar.activation(dst, area(0)[:, m], ACT.Copy, scale=sc)
                a.then_inc(t_moved[0], 1)

            g_root = roots[0]

            def group(i=None):
                c0 = first(("x", 0))
                at_chunk[0] = c0
                per = 2 * CD
                if i is not None:
                    finish_z(0, i - 1)
                to(c0 + 2, i, per)
                if i is not None:
                    finish_square(0, i - 1)
                to(c0 + 3, i, per)
                if i is not None:
                    root(g_root + 1, i - 1)
                else:
                    to(c0 + 4)
                    conv_silu("C1", cT[:], bc_silu)
                to(c0 + 7, i, per)
                if i is not None:
                    finish_y(0, i - 1)
                to(c0 + CD, i, per)
                act.wait_ge(seg_ready, lin(1, i, 1))
                nc.scalar.activation(E[:], E[:], ACT.Exp).then_inc(exp_ready, 1)
                to(c0 + CD + 4, i, per)
                conv_silu(("x", 0), xc[:], xc_silu, i)
                to(c0 + CD + 6, i, per)
                act.wait_ge(t_ready[0], lin(use(0, ("xT", 0)), i, 2))
                if i is not None:
                    act.wait_ge(gated, i)
                nc.scalar.activation(X[:], A[:, 0], ACT.Copy).then_inc(t_moved[0], 1)
                to(c0 + 2 * CD, i, per)

            group()
            with act.Fori(1, GROUPS) as g:
                group(g)
            c0 = first(("gate_b", 0))
            at_chunk[0] = c0
            finish_z(GROUPS - 1)
            to(c0 + 2)
            finish_square(GROUPS - 1)
            to(c0 + 3)
            roots[0] = g_root + GROUPS
            root(roots[0])
            to(c0 + 7)
            finish_y(GROUPS - 1)

            def yn_split(b):
                act.wait_ge(t_moved[0], use(0, ("yT", GROUPS - 1)))
                nc.scalar.activation(ynh[:, b * M:(b + 1) * M], yn[:, b * M:(b + 1) * M], ACT.Copy).then_inc(yn_high, 1)

            for j in range(NJ):
                to(end(("gate_b", j)) + 1)
                act.wait_ge(gate_biased, NJ + j + 1)
                nc.scalar.activation(sig_b[:, :, j * NCOL:(j + 1) * NCOL], sig_b[:, :, j * NCOL:(j + 1) * NCOL],
                                     ACT.Sigmoid).then_inc(gate_ready, 1)
                if j < NJ - 1:
                    for b in range(3 * j, min(3 * j + 3, GROUPS)):
                        to(end(("gate_b", j)) + 2 + b - 3 * j)
                        yn_split(b)
            for j in range(NJ):
                nxt = first(("ssd_out", j + 1)) if j < NJ - 1 else first(("mix_out", 0))
                to(nxt + 3)
                act.wait_ge(t_ready[0], use(0, ("merged", j)))
                nc.scalar.activation(uh[:, j * M:(j + 1) * M], area(0), ACT.Copy).then_inc(t_high[0], 1)
            to(first(("mix_out", 0)) + 4)
            act.wait_ge(mem_loaded, 16)
            for t in range(T):
                if t >= 1:
                    act.wait_ge(mem_squares, t)
                nc.scalar.activation(mem_junk[:], memx[:, t], ACT.Square, accum_out=ssq_res[:, t:t + 1]).then_inc(mem_squares, 1)
                to(at_chunk[0] + 1)
            next_root()
            for j in range(NJ):
                to(end(("mix_out", j)))
                done()
                job_square(("mix_out", j), NJ + j, col=slice(j, j + 1))
                marks = {0: ((1, 3, 0), (1, 6, 1)), 1: ((2, 1, 2), (2, 4, 3))}.get(j, ())
                for jj, k, q in marks:
                    to(first(("mix_out", jj)) + k)
                    split_area(0, ("mem", q), G_COL["mem"] + q * M, memh[:, q * M:(q + 1) * M])

            next_root()

            advance()
            for t in range(T):
                for h in range(2):
                    advance()
                    half_square(2, t, h)
            for t in range(T):
                next_root(slice(t, t + 1))
                advance()
            to(first("k") + 7)
            pre_high(2, 0)
            pre_high(2, 1)
            to(end("k"))
            done()
            nc.scalar.activation(kT[:], feat(slot("k")), ACT.Copy).then_inc(evacuated[slot("k")], 1)
            to(end("k") + 2)
            pre_high(2, 2)
            pre_high(2, 3)
            to(end("q"))
            done()
            nc.scalar.activation(qT[:], feat(slot("q")), ACT.Copy).then_inc(evacuated[slot("q")], 1)
            to(first("v") + 2)
            scale = float(P) ** -0.5
            for t in range(T):
                act.wait_ge(max_ready, t + 1)
                for h in range(X_HEADS):
                    n = t * X_HEADS + h
                    e = nc.scalar.activation(prob[:, t, h], area(t)[:, h], ACT.Exp, bias=smax[:, 1, n:n + 1], scale=scale,
                                             accum_out=smax[:, 2, n:n + 1])
                e.then_inc(probs, 1)
                advance()
            to(first("v") + 7)
            for mt in range(T):
                act.wait_ge(t_ready[mt], use(mt, f"probT{mt}"))
                nc.scalar.activation(probT[:, mt], area(mt), ACT.Copy).then_inc(t_moved[mt], 1)
            to(end("v"))
            done()
            nc.scalar.activation(V[:, :, 0:2 * P], tok(slot("v"))[:, :, 0:2 * P], ACT.Copy).then_inc(v_moved, 1)
            nc.scalar.activation(V[:, :, 2 * P:], tok(slot("v"))[:, :, 2 * P:], ACT.Copy).then_inc(evacuated[slot("v")], 1)
            for b in range(2):
                act.wait_ge(attended, b + 1)
                nc.scalar.activation(oh[:, 2 * b:2 * b + 2], feat(slot("attend"))[:, 2 * b:2 * b + 2], ACT.Copy).then_inc(o_high, 1)
            for j in range(NJ):
                if j == 0:
                    to(end(("xo", 0)) - 1)
                    fetch_root(3)
                to(end(("xo", j)))
                done()
                job_square(("xo", j), 2 * NJ + j, col=slice(j, j + 1))
            next_root()
            pre_norm_behind(3)
            ffn(1)
            next_root()

        @block.vector
        def _(dve):
            at_chunk = [0]
            steps = [0]
            loop = [None, 0]

            def link(ins):
                steps[0] += 1
                ins.then_inc(step, 1)
                dve.wait_ge(step, lin(steps[0], *loop))

            def advance(i=None, per=0):
                c = at_chunk[0] + AHEAD
                at_chunk[0] += 1
                if c < NCH:
                    r = c % RING
                    dve.wait_ge(high, lin(c + 1, i, per))
                    nc.vector.tensor_tensor(wl[:, r], raw[:, r], wh[:, r].bitcast(F32), ALU.subtract).then_inc(low, 1)

            def to(n, i=None, per=0):
                assert at_chunk[0] <= n, (at_chunk[0], n)
                while at_chunk[0] < n:
                    advance(i, per)

            def done(i=None, per=0):
                dve.wait_ge(used, lin(at_chunk[0], i, per))

            def first_split(r):
                dve.wait_ge(high, r + 1)
                nc.vector.tensor_tensor(wl[:, r], raw[:, r], wh[:, r].bitcast(F32), ALU.subtract).then_inc(low, 1)

            roots = [0]

            def inv_root(total, n_elem, ap=slice(0, T)):
                roots[0] += 1
                nc.vector.tensor_scalar(sv[:, ap], total, 1.0 / n_elem, EPS, ALU.mult, ALU.add).then_inc(var_ready, 1)
                dve.wait_ge(root_ready, roots[0])
                link(nc.vector.reciprocal(sr[:, ap], ss[:, ap]))

            def row_wait(name, i=None):
                dve.wait_ge(row_loaded[slot(name)], lin(16 * row_count(name), i, 16))

            def gained(name, n, i=None, col=None, last=None):
                dve.wait_ge(job_squares, n)
                if last is not None:
                    post_var(last)
                gain_product(name, i, col)

            def gain_product(name, i, col):
                row_wait(name, i)
                nc.vector.tensor_tensor(F[:, :, col], tok(slot(name)),
                                        row_bc[:, slot(name)].unsqueeze(1).to_broadcast([P, T, NCOL]),
                                        ALU.mult).then_inc(evacuated[slot(name)], 1)

            def post_var(factor):
                link(nc.vector.tensor_reduce(ssum, ssq_job, AX.X, ALU.add))
                f = factor ** -2
                nc.vector.tensor_scalar(sv, ssum, f / D, f * EPS, ALU.mult, ALU.add).then_inc(var_ready, 1)

            def update(n, t, c):
                nc.vector.scalar_tensor_tensor(out=res[:, t, c], in0=F[:, t, c], scalar=sr[:, t:t + 1], in1=res[:, t, c],
                                               op0=ALU.mult, op1=ALU.add).then_inc(res_ready, 1)

            def post_norm(n, last_name, pause=lambda: None, between=lambda q: None):
                if n != 3:
                    dve.wait_ge(evacuated[slot(last_name)], moved(last_name))
                roots[0] += 1
                dve.wait_ge(root_ready, roots[0])
                link(nc.vector.reciprocal(sr, ss))
                pause()
                if UPDATES[n] == NJ * T:
                    for q in range(NJ):
                        if q == NJ - 1:
                            gain_product(last_name, None, slice(q * NCOL, (q + 1) * NCOL))
                            dve.wait_ge(evacuated[slot(last_name)], moved(last_name))
                        for t in range(T):
                            update(n, t, slice(q * NCOL, (q + 1) * NCOL))
                        if q >= NJ - 2:
                            between(q - (NJ - 2))
                else:
                    for t in range(T):
                        for q in range(2):
                            update(n, t, slice(q * D // 2, (q + 1) * D // 2))
                            pause()

            def low_area(k, name, gain, hi, dst):
                for m in range(M):
                    if m % 2 == 0:
                        dve.wait_ge(t_high[k], high_use(k, name) - 1 + m // 2)
                    l = nc.vector.scalar_tensor_tensor(out=dst[:, m], in0=area(k)[:, m], scalar=cols[:, gain + m:gain + m + 1],
                                                       in1=hi[:, m].bitcast(F32), op0=ALU.mult, op1=ALU.subtract)
                l.then_inc(t_moved[k], 1)

            def pre_low(n, q):
                low_area(q % 2, (f"pre{n}", q), G_COL[f"pre{n}"] + q * M, uh[:, q * M:(q + 1) * M], ul[:, q * M:(q + 1) * M])

            def pre_scale(n, pause=lambda: None):
                for t in range(T):
                    dve.wait_ge(res_squares, squares_before(n) + 2 * (t + 1))
                    link(nc.vector.tensor_tensor(ssq_res[:, t:t + 1], ssq_half[:, t, 0:1], ssq_half[:, t, 1:2], ALU.add))
                    inv_root(ssq_res[:, t:t + 1], D, ap=slice(t, t + 1))
                    nc.vector.tensor_scalar(diag[:, t], ident[:], sr[:, t:t + 1], None, ALU.mult).then_inc(normed, 1)
                    pause()

            def pre_norm(n):
                pre_scale(n)
                for q in range(4):
                    pre_low(n, q)

            def pre_norm_behind(n, first_splits=lambda r: None):
                if n == 0:
                    for q in range(2):
                        first_splits(q)
                        pre_low(n, q)
                    first_splits(2)
                advance()
                pre_low(n, 2)
                advance()
                pre_low(n, 3)
                if n == 0:
                    dve.wait_ge(cols_ready, 3)
                    nc.vector.tensor_copy(cols[:, KD:], J[:, 1, 0, KD:368]).then_inc(cols_ready, 1)
                advance()
                dve.wait_ge(res_squares, squares_before(n) + T)
                roots[0] += 1
                nc.vector.tensor_scalar(sv, ssq_res, 1.0 / D, EPS, ALU.mult, ALU.add).then_inc(var_ready, 1)
                dve.wait_ge(root_ready, roots[0])
                nc.vector.reciprocal(sr_ffn, ss).then_inc(normed, 1)

            def ffn(f):
                c0 = first(("gate", f, 0))
                g, u = ("gate", f, 0), ("up", f, 0)

                def hidden_low(i=None, j=0):
                    dve.wait_ge(t_high[0], lin(high_use(0, ("hidden", f, j)), i, 1))
                    sl = slice(j * M, (j + 1) * M) if i is None else bass.ds(i * M, M)
                    nc.vector.tensor_tensor(hidl[:, sl], area(0), hidh[:, sl].bitcast(F32), ALU.subtract).then_inc(t_moved[0], 1)

                def pair(i=None):
                    if i is not None:
                        at_chunk[0] = c0
                    to(c0 + 3, i, 2 * CD)
                    if i is not None:
                        hidden_low(i - 1)
                    to(c0 + 2 * CD, i, 2 * CD)
                    done(i, 2 * CD)
                    dve.wait_ge(evacuated[slot(g)], lin(moved(g), i, 1))
                    for t in range(T):
                        h = nc.vector.scalar_tensor_tensor(out=hid[:, t], in0=tok(slot(u))[:, t], scalar=sr_ffn[:, t:t + 1],
                                                           in1=silu_g[:, t], op0=ALU.mult, op1=ALU.mult)
                    h.then_inc(evacuated[slot(u)], 1)

                pair()
                with dve.Fori(1, NP) as j:
                    pair(j)
                at_chunk[0] = first(("down", f, 0))
                hidden_low(None, NP - 1)
                d0 = first(("down", f, 0))
                if f == 0:
                    with dve.Fori(0, NJ // 2) as i:
                        at_chunk[0] = d0
                        for o in range(2):
                            to(d0 + (o + 1) * CF, i, 2 * CF)
                            gained(("down", f, o), i * 2 + (o + 1), i, bass.ds(i * (2 * NCOL) + o * NCOL, NCOL))
                    at_chunk[0] = end(("down", f, NJ - 1))
                else:
                    for j in range(NJ):
                        to(end(("down", f, j)))
                        gained(("down", f, j), 3 * NJ + j + 1, col=slice(j * NCOL, (j + 1) * NCOL),
                               last=0.5 if j == NJ - 1 else None)

            dve.wait_ge(cols_ready, 1)
            nc.vector.tensor_copy(cols[:, 0:KD], J[:, 0, 0, 0:KD]).then_inc(cols_ready, 1)
            pre_norm_behind(0, first_split)
            ffn(0)
            dve.wait_ge(job_squares, NJ)
            post_var(0.5)
            post_norm(1, ("down", 0, NJ - 1))
            pre_norm(1)

            def pool_window(g):
                dve.wait_ge(evacuated[slot(f"pin{g}")], moved(f"pin{g}"))
                if g >= 1:
                    dve.wait_ge(pooled_high, g)
                dve.wait_ge(step, steps[0])
                src = pool_x
                for n in range(g + 1):
                    dst = (win_a, win_b)[n % 2]
                    sh = 1 << n
                    nc.vector.tensor_copy(dst[:, :, 0:sh], src[:, :, 0:sh])
                    link(nc.vector.tensor_tensor(dst[:, :, sh:S], src[:, :, sh:S], src[:, :, 0:S - sh], ALU.add))
                    src = dst
                    if n == 1:
                        advance()
                link(nc.vector.tensor_tensor(win_b[:], src[:], invc[:, g].unsqueeze(1).to_broadcast([P, M, S]), ALU.mult))
                nc.vector.tensor_tensor(win_a[:], win_b[:], pool_x[:], ALU.subtract).then_inc(pooled_ready, 1)

            def pool_low(g):
                dve.wait_ge(pooled_high, g + 1)
                nc.vector.tensor_tensor(pooll[:], win_a[:], poolh[:].bitcast(F32), ALU.subtract).then_inc(pooled_low, 1)

            def pool_mixed(g):
                to(end(f"pw{g}"))
                dve.wait_ge(pw_high, g + 1)
                for m in range(M):
                    c = PS_COL + g * M + m
                    l = nc.vector.scalar_tensor_tensor(out=mixl[:, g * M + m], in0=feat(slot(f"pw{g}"))[:, m],
                                                       scalar=cols[:, c:c + 1], in1=mixh[:, g * M + m].bitcast(F32),
                                                       op0=ALU.mult, op1=ALU.subtract)
                l.then_inc(evacuated[slot(f"pw{g}")], 1)

            def conv(name, dst, blk, i=None, per=0, blk_per=0, pause=True):
                done(i, per)
                nb = CONV // P
                o = feat(slot(name))

                def col(tap, m):
                    c = CW_COL + tap * nb + blk + m if tap is not None else CB_COL + blk + m
                    return cols[:, c:c + 1] if i is None else cols[:, bass.ds(i * blk_per + c, 1)]

                for m in range(M):
                    l = nc.vector.tensor_scalar(dst[:, m], o[:, m], col(TAPS - 1, m), col(None, m), ALU.mult, ALU.add)
                link(l)
                for sh in range(1, TAPS):
                    for m in range(M):
                        l = nc.vector.scalar_tensor_tensor(out=dst[:, m, sh:S], in0=o[:, m, 0:S - sh], scalar=col(TAPS - 1 - sh, m),
                                                           in1=dst[:, m, sh:S], op0=ALU.mult, op1=ALU.add)
                    if sh < TAPS - 1:
                        link(l)
                    else:
                        l.then_inc(evacuated[slot(name)], 1)
                    if pause:
                        advance(i, per)

            to(end("pin0"))
            dve.wait_ge(mix_loaded, 64)
            pool_window(0)
            to(end("dt"))
            done()
            nc.vector.tensor_copy(dt_rows[:], J[0:HEADS, slot("dt"), 0, 0:S]).then_inc(evacuated[slot("dt")], 1)
            to(end("dt") + 2)
            dve.wait_ge(mix_loaded, 64)
            dve.wait_ge(t_ready[1], use(1, "dt"))
            dtr, ab, ex, lg, dtv, av = (small[:, n:n + T] for n in (DTR, AB, EX, LG, DTV, AV))
            nc.vector.tensor_tensor(dtr, A[:, 1, 0, 0:T * HEADS].rearrange("p (t h) -> p t h", t=T),
                                    dtb_bc[:].unsqueeze(1).to_broadcast([P, T, HEADS]), ALU.add).then_inc(t_moved[1], 1)
            to(end("dt") + 3)
            dve.wait_ge(dt_func, 3)
            nc.vector.tensor_scalar(ab, ex, 1.0, None, ALU.add).then_inc(dt_step, 1)
            dve.wait_ge(dt_step, 1)
            dve.wait_ge(dt_func, 4)
            link(nc.vector.tensor_scalar(ab, ab, -1.0, None, ALU.add))
            link(nc.vector.tensor_scalar(dtv, ab, 1e-7, None, ALU.max))
            link(nc.vector.reciprocal(dtv, dtv))
            link(nc.vector.tensor_tensor(lg, lg, ex, ALU.mult))
            link(nc.vector.tensor_tensor(lg, lg, dtv, ALU.mult))
            link(nc.vector.scalar_tensor_tensor(out=dtv, in0=ab, scalar=0.0, in1=ex, op0=ALU.is_equal, op1=ALU.mult))
            link(nc.vector.tensor_tensor(lg, lg, dtv, ALU.add))
            link(nc.vector.scalar_tensor_tensor(out=dtv, in0=dtr, scalar=0.0, in1=lg, op0=ALU.max, op1=ALU.add))
            nc.vector.scalar_tensor_tensor(out=av, in0=dtv, scalar=-1.0, in1=small[:, EA].unsqueeze(1).to_broadcast([P, T, HEADS]),
                                           op0=ALU.mult, op1=ALU.mult).then_inc(a_ready, 1)
            pool_low(0)
            to(first("pin1") + 7)
            dve.wait_ge(t_ready[1], use(1, "cs"))
            link(nc.vector.tensor_copy(small[:, REM], A[:, 1, 1, 0:HEADS]))
            nc.vector.tensor_copy(small[:, CS:CS + T], A[:, 1, 0, 0:T * HEADS].rearrange("p (t h) -> p t h", t=T)).then_inc(t_moved[1], 1)

            to(end("pin1"))
            pool_window(1)
            dve.wait_ge(t_ready[1], use(1, "csT"))
            nc.vector.tensor_copy(cst[:], A[:, 1, 0, 0:P]).then_inc(t_moved[1], 1)
            pool_mixed(0)
            to(end("pw0") + 3)
            pool_low(1)
            to(end("pin2"))
            pool_window(2)
            pool_mixed(1)
            to(end("pw1") + 3)
            pool_low(2)
            to(end("pin3"))
            pool_window(3)
            pool_mixed(2)
            to(end("pw2") + 3)
            pool_low(3)
            to(end("B0"))
            conv("B0", bT, INNER // P, pause=False)
            pool_mixed(3)
            c0 = first(("gate_a", 0))
            with dve.Fori(0, NJ) as j:
                at_chunk[0] = c0
                loop[0] = j
                loop[1] = 0
                to(c0 + CD, j, 2 * CD)
                done(j, 2 * CD)
                row_wait(("gate_a", 0), j)
                nc.vector.tensor_tensor(sig_a[:], tok(slot(("gate_a", 0))),
                                        row_bc[:, slot(("gate_a", 0))].unsqueeze(1).to_broadcast([P, T, NCOL]),
                                        ALU.add).then_inc(gate_biased, 1)
                dve.wait_ge(gate_biased, j + 1)
                dve.sem_inc(evacuated[slot(("gate_a", 0))], 1)
                to(c0 + 2 * CD, j, 2 * CD)
                done(j, 2 * CD)
                dve.wait_ge(gate_ready, j + 1)
                nc.vector.tensor_tensor(F[:, :, bass.ds(j * NCOL, NCOL)], tok(slot(("pool_out", 0))), sig_a[:],
                                        ALU.mult).then_inc(merged, 1)
                dve.wait_ge(merged, j + 1)
                dve.sem_inc(evacuated[slot(("pool_out", 0))], 1)
            loop[0] = None
            at_chunk[0] = first("C0")
            to(end("C0"))
            conv("C0", cT, INNER // P + GROUPS)

            def cb_masked(half, pair):
                dve.wait_ge(t_ready[1], use(1, ("cb", 2 * half + pair)))
                for q in range(2):
                    g = 4 * half + 2 * pair + q
                    nc.vector.tensor_tensor(cbm[:, g, 0:P], A[:, 1, q, 0:P], tri[:], ALU.mult)
                    nc.vector.tensor_copy(cbm[:, g, P:2 * P], A[:, 1, q, P:2 * P])
                    l = nc.vector.tensor_tensor(cbm[:, g, 2 * P:3 * P], A[:, 1, q, 2 * P:3 * P], tri[:], ALU.mult)
                l.then_inc(t_moved[1], 1)

            to(first("B1") + 5)
            cb_masked(0, 0)
            to(first("B1") + 6)
            cb_masked(0, 1)
            to(end("B1"))
            conv("B1", bT, INNER // P + M)
            to(end("C1"))

            def heads(ap):
                return ap.rearrange("p t (h e) -> p t h e", h=HPG)

            def finish_gate(g0, i=None):
                dve.wait_ge(t_ready[1], lin(use(1, ("Y", g0)), i, 1))
                nc.vector.tensor_tensor(yb[:], A[:, 1], yb[:], ALU.add).then_inc(t_moved[1], 1)
                dve.wait_ge(t_moved[1], lin(use(1, ("Y", g0)), i, 1))
                dve.wait_ge(evacuated[slot(("z", 0))], lin(moved(("z", g0)), i, 1))
                nc.vector.tensor_tensor(yb[:], yb[:], zs[:], ALU.mult).then_inc(gated, 1)

            def finish_var(g0, i=None):
                dve.wait_ge(y_squares, lin(g0 + 1, i, 1))
                nc.vector.tensor_scalar(sv, ssq_res, 1.0 / WG, EPS, ALU.mult, ALU.add).then_inc(var_ready, 1)

            def finish_scale(g0, i=None):
                dve.wait_ge(root_ready, lin(g_root + g0 + 1, i, 1))
                link(nc.vector.reciprocal(sr, ss))
                for t in range(T):
                    l = nc.vector.tensor_scalar(yb[:, t], yb[:, t], sr[:, t:t + 1], None, ALU.mult)
                l.then_inc(y_normed, 1)

            g_root = roots[0]
            GROUP_STEPS = 5
            step0 = steps[0]

            def group(i=None):
                c0 = first(("x", 0))
                at_chunk[0] = c0
                per = 2 * CD
                steps[0] = step0 if i is None else step0 + 2
                loop[0], loop[1] = i, GROUP_STEPS
                if i is None:
                    dve.wait_ge(used, c0)
                    dve.wait_ge(t_moved[1], use(1, ("cb", 1)))
                    conv("C1", cT, INNER // P + GROUPS + M)
                else:
                    to(c0 + 1, i, per)
                    finish_gate(0, i - 1)
                    to(c0 + 3, i, per)
                    finish_var(0, i - 1)
                    to(c0 + 4, i, per)
                    finish_scale(0, i - 1)
                if i is None:
                    to(c0 + 6)
                    cb_masked(1, 0)
                to(c0 + 7, i, per)
                if i is None:
                    cb_masked(1, 1)
                    dve.wait_ge(t_moved[1], use(1, ("cb", 3)))
                dve.wait_ge(csb_loaded, lin(16 * T, i, 16 * T))
                for h in range(HPG):
                    def scalar(row):
                        return small[:, row, h:h + 1] if i is None else small[:, row, bass.ds(i * HPG + h, 1)]
                    nc.vector.tensor_scalar(E[:, h, 0:P], csb[:, h, 0], scalar(CS), 0.0, ALU.subtract, ALU.min)
                    nc.vector.tensor_scalar(E[:, h, P:2 * P], csb[:, h, 1], scalar(REM), 0.0, ALU.add, ALU.min)
                    l = nc.vector.tensor_scalar(E[:, h, 2 * P:3 * P], csb[:, h, 1], scalar(CS + 1), 0.0, ALU.subtract, ALU.min)
                l.then_inc(seg_ready, 1)
                to(c0 + CD, i, per)
                conv(("x", 0), xc, 0, i, per, M)
                to(c0 + CD + 4, i, per)
                dve.wait_ge(exp_ready, lin(1, i, 1))
                c = cbm[:, 0:1] if i is None else cbm[:, bass.ds(i, 1)]
                nc.vector.tensor_tensor(E[:], E[:], c.to_broadcast([P, HPG, 3 * P]), ALU.mult).then_inc(w_ready, 1)
                to(c0 + CD + 6, i, per)
                dve.wait_ge(t_moved[0], lin(use(0, ("xT", 0)), i, 2))
                dt_sl = slice(0, HPG) if i is None else bass.ds(i * HPG, HPG)
                nc.vector.tensor_tensor(heads(Xdt[:]), heads(X[:]), small[:, DTV:DTV + T, dt_sl].unsqueeze(3).to_broadcast([P, T, HPG, HEAD_DIM]),
                                        ALU.mult).then_inc(xdt_ready, 1)
                link(nc.vector.tensor_tensor(heads(yb[:]), heads(X[:]),
                                             d_bc[:, dt_sl].unsqueeze(1).unsqueeze(3).to_broadcast([P, T, HPG, HEAD_DIM]), ALU.mult))
                to(c0 + 2 * CD, i, per)

            group()
            assert steps[0] == step0 + GROUP_STEPS + 2, steps[0] - step0
            with dve.Fori(1, GROUPS) as g:
                group(g)
            assert steps[0] == step0 + 2 + GROUP_STEPS
            steps[0] = step0 + 2 + GROUP_STEPS * GROUPS
            loop[0] = None
            roots[0] = g_root + GROUPS
            c0 = first(("gate_b", 0))
            at_chunk[0] = c0
            to(c0 + 1)
            finish_gate(GROUPS - 1)
            to(c0 + 3)
            finish_var(GROUPS - 1)
            to(c0 + 4)
            finish_scale(GROUPS - 1)

            def yn_split(b):
                dve.wait_ge(yn_high, b + 1)
                nc.vector.tensor_tensor(ynl[:, b * M:(b + 1) * M], yn[:, b * M:(b + 1) * M],
                                        ynh[:, b * M:(b + 1) * M].bitcast(F32), ALU.subtract).then_inc(yn_low, 1)

            for j in range(NJ):
                name = ("gate_b", j)
                to(end(name))
                done()
                row_wait(name)
                nc.vector.tensor_tensor(sig_b[:, :, j * NCOL:(j + 1) * NCOL], tok(slot(name)),
                                        row_bc[:, slot(name)].unsqueeze(1).to_broadcast([P, T, NCOL]), ALU.add).then_inc(gate_biased, 1)
                dve.wait_ge(gate_biased, NJ + j + 1)
                dve.sem_inc(evacuated[slot(name)], 1)
                if j < NJ - 1:
                    for b in range(3 * j, min(3 * j + 3, GROUPS)):
                        to(end(name) + 2 + b - 3 * j)
                        yn_split(b)
            def merged_low(j):
                dve.wait_ge(t_high[0], high_use(0, ("merged", j)))
                nc.vector.tensor_tensor(ul[:, j * M:(j + 1) * M], area(0), uh[:, j * M:(j + 1) * M].bitcast(F32),
                                        ALU.subtract).then_inc(t_moved[0], 1)

            for j in range(NJ):
                name = ("ssd_out", j)
                if j >= 1:
                    to(first(name) + 3)
                    merged_low(j - 1)
                to(end(name))
                done()
                dve.wait_ge(gate_ready, NJ + j + 1)
                sg = sig_b[:, :, j * NCOL:(j + 1) * NCOL]
                Fj = F[:, :, j * NCOL:(j + 1) * NCOL]
                nc.vector.tensor_tensor(sg, tok(slot(name)), sg, ALU.mult).then_inc(evacuated[slot(name)], 1)
                dve.wait_ge(evacuated[slot(name)], moved(name))
                nc.vector.tensor_tensor(Fj, Fj, sg, ALU.add).then_inc(merged, 1)
            to(first(("mix_out", 0)) + 3)
            merged_low(NJ - 1)
            to(first(("mix_out", 0)) + 6)
            dve.wait_ge(mem_squares, T)
            inv_root(ssq_res, D)
            for t in range(T):
                nc.vector.tensor_scalar(memx[:, t], memx[:, t], sr[:, t:t + 1], None, ALU.mult).then_inc(mem_normed, 1)
            for j in range(NJ):
                to(end(("mix_out", j)))
                gained(("mix_out", j), NJ + j + 1, col=slice(j * NCOL, (j + 1) * NCOL), last=1.0 if j == NJ - 1 else None)
                for jj, k, q in {0: ((1, 3, 0), (1, 6, 1)), 1: ((2, 1, 2), (2, 4, 3))}.get(j, ()):
                    to(first(("mix_out", jj)) + k)
                    low_area(0, ("mem", q), G_COL["mem"] + q * M, memh[:, q * M:(q + 1) * M], meml[:, q * M:(q + 1) * M])

            post_norm(2, ("mix_out", NJ - 1), pause=advance)
            pre_scale(2, advance)
            to(first("k") + 7)
            pre_low(2, 0)
            pre_low(2, 1)
            to(end("k") + 2)
            pre_low(2, 2)
            pre_low(2, 3)
            to(first("v") + 1)
            scale = float(P) ** -0.5
            for t in range(T):
                n = slice(t * X_HEADS, (t + 1) * X_HEADS)
                dve.wait_ge(t_ready[t], use(t, f"score{t}"))
                link(nc.vector.tensor_reduce(smax[:, 0, n], area(t), AX.X, ALU.max))
                nc.vector.tensor_scalar(smax[:, 1, n], smax[:, 0, n], -scale, None, ALU.mult).then_inc(max_ready, 1)
            for t in range(T):
                advance()
                advance()
                n = slice(t * X_HEADS, (t + 1) * X_HEADS)
                dve.wait_ge(probs, t + 1)
                dve.sem_inc(t_moved[t], 1)
                link(nc.vector.reciprocal(smax[:, 3, n], smax[:, 2, n]))
                nc.vector.tensor_tensor(prob[:, t], prob[:, t], smax[:, 3, n].unsqueeze(2).to_broadcast([P, X_HEADS, S]),
                                        ALU.mult).then_inc(probs_scaled, 1)
            to(end("v"))
            for b in range(2):
                dve.wait_ge(o_high, b + 1)
                h = slice(2 * b, 2 * b + 2)
                o = nc.vector.tensor_tensor(ol[:, h], feat(slot("attend"))[:, h], oh[:, h].bitcast(F32), ALU.subtract)
                o.then_inc((o_low, evacuated[slot("attend")])[b], 1)
            for j in range(NJ):
                to(end(("xo", j)))
                if j < NJ - 1:
                    gained(("xo", j), 2 * NJ + j + 1, col=slice(j * NCOL, (j + 1) * NCOL))
            dve.wait_ge(job_squares, 3 * NJ)
            post_var(1.0)
            dve.wait_ge(evacuated[slot(("xo", NJ - 2))], moved(("xo", NJ - 2)))
            post_norm(3, ("xo", NJ - 1), between=lambda q: pre_low(3, q))
            pre_norm_behind(3)
            ffn(1)
            post_norm(4, ("down", 1, NJ - 1))


_INS = ["x", "mem", "ffn1_pre_g", "ffn1_w1", "ffn1_w3", "ffn1_w2", "ffn1_post_g", "mix_pre_g", "w_in", "b_gate",
        "pool_w", "pool_scale", "w_pool_out", "conv_w", "conv_b", "dt_bias", "a_log", "d_skip", "ssd_norm_g",
        "w_ssd_out", "w_mix_out", "mix_post_g", "xattn_pre_g", "mem_norm_g", "w_q", "w_k", "w_v", "w_xo",
        "xattn_post_g", "ffn2_pre_g", "ffn2_w1", "ffn2_w3", "ffn2_w2", "ffn2_post_g"]


def kernel(**inputs):
    import numpy as _np
    import concourse.bacc as _bacc
    from concourse import mybir as _mybir
    from concourse.bass_utils import run_bass_kernel_spmd as _run

    seq = inputs["x"].shape[1]
    consts = {
        "identity": _np.eye(P, dtype=_np.float32),
        "causal": _np.triu(_np.ones((P, P), _np.float32)),
        "anticausal": _np.tril(_np.ones((P, P), _np.float32), -1),
        "inv_count": _np.stack([1.0 / _np.minimum(_np.arange(seq) + 1, w) for w in WINDOWS]).astype(_np.float32),
    }
    nc = _bacc.Bacc("TRN2", target_bir_lowering=False, num_devices=1)
    arrays, args = {}, []
    for name in _INS + list(consts):
        a = _np.ascontiguousarray(consts[name] if name in consts else inputs[name])
        arrays[f"in_{name}_dram"] = a
        args.append(nc.dram_tensor(f"in_{name}_dram", a.shape, _mybir.dt.from_np(a.dtype), kind="ExternalInput").ap())
    shape = inputs["x"].shape
    args.append(nc.dram_tensor("out_0_dram", shape, _mybir.dt.float32, kind="ExternalOutput").ap())
    hybrid_block(nc, *args)
    r = _run(nc, [arrays], core_ids=[0])
    return r.results[0]["out_0_dram"]
```
